# Optimizing a Trainium2 kernel written in Bass

```python
import math
import jax, jax.numpy as jnp
from jax import lax
import numpy as np

D_MODEL = 1024
BATCH = 1
SEQ = 256
DEPTH = 1

HEAD_DIM = 64
N_DIFF_HEADS = D_MODEL // 2 // (2 * HEAD_DIM)
DIFF_WIDTH = N_DIFF_HEADS * 2 * HEAD_DIM
N_DIL_HEADS = D_MODEL // 2 // HEAD_DIM
DIL_WIDTH = N_DIL_HEADS * HEAD_DIM
MIX_WIDTH = DIFF_WIDTH + DIL_WIDTH
DIL_PATTERNS = ((128, 1), (512, 4), (2048, 16))
N_BUCKETS = 32
REL_MAX_DIST = 1024
Q_BLOCK = 128
N_EXPERTS = 16
EC_K = 2
D_FF = 256 * ((8 * D_MODEL // 3 + 255) // 256)
NORM_EPS = 1e-6
SUBLN_EPS = 1e-5
NEG = -1e30


def rms_norm(x, g, eps=NORM_EPS):
    xf = x.astype(jnp.float32)
    y = xf * lax.rsqrt(jnp.mean(xf * xf, axis=-1, keepdims=True) + eps)
    return (y * g.astype(jnp.float32)).astype(x.dtype)

def t5_bucket(rel):
    half = N_BUCKETS // 2
    max_exact = half // 2
    n = jnp.abs(rel)
    nf = jnp.maximum(n, 1).astype(jnp.float32)
    large = max_exact + (jnp.log(nf / max_exact) / math.log(REL_MAX_DIST / max_exact)
                         * (half - max_exact)).astype(jnp.int32)
    large = jnp.minimum(large, half - 1)
    return jnp.where(rel > 0, half, 0) + jnp.where(n < max_exact, n, large)

def diff_attention(qa, ka, va, lam, lambda_init, subln_g, bias_a):
    B, S = qa.shape[:2]
    H = N_DIFF_HEADS
    q = qa.reshape(B, S, H, 2, HEAD_DIM) * (HEAD_DIM ** -0.5)
    k = ka.reshape(B, S, H, 2, HEAD_DIM)
    k1 = k[:, :, :, 0].transpose(0, 2, 1, 3)
    k2 = k[:, :, :, 1].transpose(0, 2, 1, 3)
    v = va.reshape(B, S, H, 2 * HEAD_DIM).transpose(0, 2, 1, 3)
    n_blk = S // Q_BLOCK

    def to_qblocks(t):
        return t.reshape(B, n_blk, Q_BLOCK, H, HEAD_DIM).transpose(1, 0, 3, 2, 4)

    q1b = to_qblocks(q[:, :, :, 0])
    q2b = to_qblocks(q[:, :, :, 1])
    kpos = jnp.arange(S, dtype=jnp.int32)

    def block(args):
        j, q1, q2 = args
        qpos = j * Q_BLOCK + jnp.arange(Q_BLOCK, dtype=jnp.int32)
        bias = jnp.take(bias_a, t5_bucket(kpos[None, :] - qpos[:, None]), axis=0)
        bias = bias.transpose(2, 0, 1).astype(jnp.float32)[None]
        s1 = jnp.einsum('bhqd,bhkd->bhqk', q1, k1).astype(jnp.float32) + bias
        s2 = jnp.einsum('bhqd,bhkd->bhqk', q2, k2).astype(jnp.float32) + bias
        p = jax.nn.softmax(s1, axis=-1) - lam * jax.nn.softmax(s2, axis=-1)
        return jnp.einsum('bhqk,bhkd->bhqd', p.astype(v.dtype), v)

    o = lax.map(block, (jnp.arange(n_blk, dtype=jnp.int32), q1b, q2b))
    o = o.transpose(1, 0, 3, 2, 4).reshape(B, S, H, 2 * HEAD_DIM)
    o = rms_norm(o, subln_g, SUBLN_EPS) * (1.0 - lambda_init)
    return o.reshape(B, S, DIFF_WIDTH)

def dilated_pattern(q, k, v, window, dil, bias_b):
    B, S, H, Dh = q.shape
    half = window // (2 * dil)
    blk = half
    unit = dil * blk
    sp = -(-S // unit) * unit
    m_len = sp // dil
    nb = m_len // blk

    def to_blocks(t):
        t = jnp.pad(t, ((0, 0), (0, sp - S), (0, 0), (0, 0)))
        t = t.reshape(B, m_len, dil, H, Dh).transpose(0, 2, 3, 1, 4)
        return t.reshape(B, dil, H, nb, blk, Dh)

    def with_neighbours(t):
        tp = jnp.pad(t, ((0, 0), (0, 0), (0, 0), (1, 1), (0, 0), (0, 0)))
        return jnp.concatenate([tp[:, :, :, :-2], tp[:, :, :, 1:-1], tp[:, :, :, 2:]], axis=4)

    qb = to_blocks(q * (Dh ** -0.5))
    kn = with_neighbours(to_blocks(k))
    vn = with_neighbours(to_blocks(v))
    off = (jnp.arange(3 * blk, dtype=jnp.int32)[None, :] - blk
           - jnp.arange(blk, dtype=jnp.int32)[:, None])
    in_band = jnp.abs(off) <= half
    m_key = (jnp.arange(nb, dtype=jnp.int32)[:, None] * blk
             + jnp.arange(3 * blk, dtype=jnp.int32)[None, :] - blk)
    pos_key = m_key[None] * dil + jnp.arange(dil, dtype=jnp.int32)[:, None, None]
    key_ok = (m_key >= 0)[None] & (pos_key < S)
    mask = key_ok[:, :, None, :] & in_band[None, None]
    bias = jnp.take(bias_b, t5_bucket(off * dil), axis=0).transpose(2, 0, 1).astype(jnp.float32)
    s = jnp.einsum('brhnqd,brhnkd->brhnqk', qb, kn).astype(jnp.float32) + bias[None, None, :, None]
    s = jnp.where(mask[None, :, None], s, NEG)
    lse = jax.nn.logsumexp(s, axis=-1)
    p = jnp.exp(s - lse[..., None])
    o = jnp.einsum('brhnqk,brhnkd->brhnqd', p.astype(v.dtype), vn)
    o = o.reshape(B, dil, H, m_len, Dh).transpose(0, 3, 1, 2, 4).reshape(B, sp, H, Dh)[:, :S]
    lse = lse.reshape(B, dil, H, m_len).transpose(0, 3, 1, 2).reshape(B, sp, H)[:, :S]
    return o, lse

def dilated_attention(qd, kd, vd, bias_b):
    B, S = qd.shape[:2]
    q = qd.reshape(B, S, N_DIL_HEADS, HEAD_DIM)
    k = kd.reshape(B, S, N_DIL_HEADS, HEAD_DIM)
    v = vd.reshape(B, S, N_DIL_HEADS, HEAD_DIM)
    outs, lses = [], []
    for window, dil in DIL_PATTERNS:
        o, lse = dilated_pattern(q, k, v, window, dil, bias_b)
        outs.append(o)
        lses.append(lse)
    w = jax.nn.softmax(jnp.stack(lses, axis=0), axis=0)
    o = jnp.sum(w[..., None] * jnp.stack(outs, axis=0).astype(jnp.float32), axis=0)
    return o.astype(qd.dtype).reshape(B, S, DIL_WIDTH)

def expert_choice_ffn(h, w_router, w_gate, w_up, w_down):
    B, S, D = h.shape
    cap = EC_K * S // N_EXPERTS
    aff = jax.nn.softmax((h @ w_router).astype(jnp.float32), axis=-1)
    g, idx = lax.top_k(aff.transpose(0, 2, 1), cap)
    g = g.transpose(1, 0, 2)
    idx = idx.transpose(1, 0, 2)
    b_rows = jnp.arange(B, dtype=jnp.int32)[:, None]

    def run_expert(args):
        wg, wu, wd, ie, ge = args
        xe = h[b_rows, ie]
        he = jax.nn.silu(xe @ wg) * (xe @ wu)
        return (he @ wd) * ge[..., None].astype(h.dtype)

    ye = lax.map(run_expert, (w_gate, w_up, w_down, idx, g))
    b_idx = jnp.arange(B, dtype=jnp.int32)[None, :, None]
    return jnp.zeros_like(h).at[b_idx, idx].add(ye)

def first_inputs(seed: int = 0) -> dict:
    key = jax.random.key(seed)
    ks = jax.random.split(key, 16)
    f = jnp.float32
    n_in = 3 * DIFF_WIDTH + 3 * DIL_WIDTH
    nrm = lambda k, shape, s: jax.random.normal(k, shape, f) * s
    return {
        'x': nrm(ks[0], (BATCH, SEQ, D_MODEL), 1.0),
        'norm1_g': 1.0 + nrm(ks[1], (DEPTH, D_MODEL), 0.02),
        'w_in': nrm(ks[2], (DEPTH, D_MODEL, n_in), D_MODEL ** -0.5),
        'lam_q1': nrm(ks[3], (DEPTH, HEAD_DIM), 0.1),
        'lam_k1': nrm(ks[4], (DEPTH, HEAD_DIM), 0.1),
        'lam_q2': nrm(ks[5], (DEPTH, HEAD_DIM), 0.1),
        'lam_k2': nrm(ks[6], (DEPTH, HEAD_DIM), 0.1),
        'subln_g': 1.0 + nrm(ks[7], (DEPTH, 2 * HEAD_DIM), 0.02),
        'w_out': nrm(ks[8], (DEPTH, MIX_WIDTH, D_MODEL), MIX_WIDTH ** -0.5),
        'rel_bias': nrm(ks[9], (N_BUCKETS, N_DIFF_HEADS + N_DIL_HEADS), 0.2),
        'norm2_g': 1.0 + nrm(ks[10], (DEPTH, D_MODEL), 0.02),
        'w_router': nrm(ks[11], (DEPTH, D_MODEL, N_EXPERTS), D_MODEL ** -0.5),
        'w_gate': nrm(ks[12], (DEPTH, N_EXPERTS, D_MODEL, D_FF), D_MODEL ** -0.5),
        'w_up': nrm(ks[13], (DEPTH, N_EXPERTS, D_MODEL, D_FF), D_MODEL ** -0.5),
        'w_down': nrm(ks[14], (DEPTH, N_EXPERTS, D_FF, D_MODEL), D_FF ** -0.5),
        'norm_f_g': 1.0 + nrm(ks[15], (D_MODEL,), 0.02),
    }

def first_block(x, norm1_g, w_in, lam_q1, lam_k1, lam_q2, lam_k2, subln_g, w_out, rel_bias,
              norm2_g, w_router, w_gate, w_up, w_down, norm_f_g):
    splits = [DIFF_WIDTH, 2 * DIFF_WIDTH, 3 * DIFF_WIDTH,
              3 * DIFF_WIDTH + DIL_WIDTH, 3 * DIFF_WIDTH + 2 * DIL_WIDTH]
    bias_a = rel_bias[:, :N_DIFF_HEADS]
    bias_b = rel_bias[:, N_DIFF_HEADS:]
    for l in range(DEPTH):
        lambda_init = 0.8 - 0.6 * math.exp(-0.3 * l)
        h = rms_norm(x, norm1_g[l])
        proj = h @ w_in[l]
        qa, ka, va, qd, kd, vd = jnp.split(proj, splits, axis=-1)
        lam = (jnp.exp(jnp.sum(lam_q1[l].astype(jnp.float32) * lam_k1[l].astype(jnp.float32)))
               - jnp.exp(jnp.sum(lam_q2[l].astype(jnp.float32) * lam_k2[l].astype(jnp.float32)))
               + lambda_init)
        oa = diff_attention(qa, ka, va, lam, lambda_init, subln_g[l], bias_a)
        od = dilated_attention(qd, kd, vd, bias_b)
        x = x + jnp.concatenate([oa, od], axis=-1) @ w_out[l]
        x = x + expert_choice_ffn(rms_norm(x, norm2_g[l]), w_router[l], w_gate[l], w_up[l], w_down[l])
    return rms_norm(x, norm_f_g)


DEPTH_2 = 2

GRID_W = 64
CTX_LEN = 256
N_MIXERS = 3
ROPE_THETA = 10000.0
LN_EPS = 1e-5
RMS_EPS = 1e-6
D_FF_2 = 4 * D_MODEL

MLA_HEADS = 8
MLA_Q_RANK = 512
MLA_KV_RANK = 256
MLA_NOPE = 128
MLA_ROPE = 64
MLA_V = 128

NA_HEADS = 16
NA_HEAD_DIM = D_MODEL // NA_HEADS
NA_WIN_ROWS = 8
NA_WIN_COLS = 16

GQA_HEAD_DIM = 128
GQA_Q_HEADS = D_MODEL // GQA_HEAD_DIM
GQA_KV_HEADS = GQA_Q_HEADS // 4
GQA_GROUP = GQA_Q_HEADS // GQA_KV_HEADS


def _layer_norm(x, g, b):
    xf = x.astype(jnp.float32)
    mu = jnp.mean(xf, -1, keepdims=True)
    var = jnp.mean(jnp.square(xf - mu), -1, keepdims=True)
    return ((xf - mu) * lax.rsqrt(var + LN_EPS) * g + b).astype(x.dtype)

def _rms_norm(x, g):
    xf = x.astype(jnp.float32)
    return (xf * lax.rsqrt(jnp.mean(xf * xf, -1, keepdims=True) + RMS_EPS) * g).astype(x.dtype)

def _rope_1d(x, pos):
    half = x.shape[-1] // 2
    freqs = ROPE_THETA ** (-jnp.arange(half, dtype=jnp.float32) / half)
    ang = pos.astype(jnp.float32)[:, None, None] * freqs
    cos, sin = jnp.cos(ang), jnp.sin(ang)
    xf = x.astype(jnp.float32)
    x1, x2 = xf[..., :half], xf[..., half:]
    return jnp.concatenate([x1 * cos - x2 * sin, x1 * sin + x2 * cos], -1).astype(x.dtype)

def _rope_2d(x, rows, cols):
    h = x.shape[-1] // 2
    return jnp.concatenate([_rope_1d(x[..., :h], rows), _rope_1d(x[..., h:], cols)], -1)

def _grid_positions(s):
    t = jnp.arange(s, dtype=jnp.int32)
    return t // GRID_W, t % GRID_W

def _block_attention(q, k, v, scale):
    b, sq, hk, g, dk = q.shape
    nb = sq // Q_BLOCK
    qb = q.reshape(b, nb, Q_BLOCK, hk, g, dk).transpose(1, 0, 2, 3, 4, 5)

    def step(qi):
        s = jnp.einsum('bqhgd,bkhd->bhgqk', qi, k).astype(jnp.float32) * scale
        p = jax.nn.softmax(s, axis=-1).astype(v.dtype)
        return jnp.einsum('bhgqk,bkhd->bqhgd', p, v)

    o = lax.map(step, qb)
    return o.transpose(1, 0, 2, 3, 4, 5).reshape(b, sq, hk * g * v.shape[-1])

def _mla_q(h, w_dq, q_norm, w_uq, rows, cols):
    b, s, _ = h.shape
    q = (_rms_norm(h @ w_dq, q_norm) @ w_uq).reshape(b, s, MLA_HEADS, MLA_NOPE + MLA_ROPE)
    q_nope, q_pe = q[..., :MLA_NOPE], q[..., MLA_NOPE:]
    if rows is not None:
        q_pe = _rope_2d(q_pe, rows, cols)
    return jnp.concatenate([q_nope, q_pe], -1)

def _mla_kv(h, w_dkv, kv_norm, w_ukv, rows, cols):
    b, s, _ = h.shape
    ckv = h @ w_dkv
    c_kv, k_pe = ckv[..., :MLA_KV_RANK], ckv[..., MLA_KV_RANK:]
    kv = (_rms_norm(c_kv, kv_norm) @ w_ukv).reshape(b, s, MLA_HEADS, MLA_NOPE + MLA_V)
    k_nope, v = kv[..., :MLA_NOPE], kv[..., MLA_NOPE:]
    k_pe = k_pe[:, :, None, :]
    if rows is not None:
        k_pe = _rope_2d(k_pe, rows, cols)
    k = jnp.concatenate([k_nope, jnp.broadcast_to(k_pe, (b, s, MLA_HEADS, MLA_ROPE))], -1)
    return k, v

def _mla_mixer(h, hc, w_dq, q_norm, w_uq, w_dkv, kv_norm, w_ukv, w_o, need_ctx):
    rows, cols = _grid_positions(h.shape[1])
    scale = (MLA_NOPE + MLA_ROPE) ** -0.5
    q = _mla_q(h, w_dq, q_norm, w_uq, rows, cols)
    k, v = _mla_kv(h, w_dkv, kv_norm, w_ukv, rows, cols)
    kc, vc = _mla_kv(hc, w_dkv, kv_norm, w_ukv, None, None)
    k_all = jnp.concatenate([kc, k], 1)
    v_all = jnp.concatenate([vc, v], 1)
    out = _block_attention(q[:, :, :, None], k_all, v_all, scale) @ w_o
    out_c = None
    if need_ctx:
        qc = _mla_q(hc, w_dq, q_norm, w_uq, None, None)
        out_c = _block_attention(qc[:, :, :, None], kc, vc, scale) @ w_o
    return out, out_c

def _na_mixer(h, hc, w_qkv, b_qkv, rpb, w_o, need_ctx):
    b, s, _ = h.shape
    n_rows = s // GRID_W
    kr = min(NA_WIN_ROWS, n_rows)
    scale = NA_HEAD_DIM ** -0.5

    def proj(t):
        qkv = (t @ w_qkv + b_qkv).reshape(t.shape[0], t.shape[1], 3, NA_HEADS, NA_HEAD_DIM)
        return qkv[:, :, 0], qkv[:, :, 1], qkv[:, :, 2]

    q, k, v = proj(h)
    qc, kc, vc = proj(hc)
    grid = (b, n_rows, GRID_W, NA_HEADS, NA_HEAD_DIM)
    q_grid, k_grid, v_grid = q.reshape(grid), k.reshape(grid), v.reshape(grid)

    r_idx = jnp.arange(n_rows, dtype=jnp.int32)
    row_start = jnp.clip(r_idx - kr // 2, 0, n_rows - kr)
    c_idx = jnp.arange(GRID_W, dtype=jnp.int32)
    col_start = jnp.clip(c_idx - NA_WIN_COLS // 2, 0, GRID_W - NA_WIN_COLS)
    col_valid = (c_idx[None, :] >= col_start[:, None]) & (c_idx[None, :] < col_start[:, None] + NA_WIN_COLS)
    mask = jnp.tile(col_valid, (1, kr))
    dc = jnp.clip(c_idx[None, :] - c_idx[:, None] + NA_WIN_COLS - 1, 0, 2 * NA_WIN_COLS - 2)
    rpb_cols = rpb[:, :, dc]

    def row_step(args):
        r, rs = args
        q_row = lax.dynamic_index_in_dim(q_grid, r, axis=1, keepdims=False)
        k_strip = lax.dynamic_slice_in_dim(k_grid, rs, kr, axis=1).reshape(b, kr * GRID_W, NA_HEADS, NA_HEAD_DIM)
        v_strip = lax.dynamic_slice_in_dim(v_grid, rs, kr, axis=1).reshape(b, kr * GRID_W, NA_HEADS, NA_HEAD_DIM)
        dr = rs + jnp.arange(kr, dtype=jnp.int32) - r + NA_WIN_ROWS - 1
        bias = jnp.take(rpb_cols, dr, axis=1).transpose(0, 2, 1, 3).reshape(NA_HEADS, GRID_W, kr * GRID_W)
        s_lat = jnp.einsum('bqhd,bkhd->bhqk', q_row, k_strip).astype(jnp.float32) * scale + bias
        s_lat = jnp.where(mask, s_lat, -jnp.inf)
        s_ctx = jnp.einsum('bqhd,bkhd->bhqk', q_row, kc).astype(jnp.float32) * scale
        p = jax.nn.softmax(jnp.concatenate([s_ctx, s_lat], -1), axis=-1).astype(v.dtype)
        return jnp.einsum('bhqk,bkhd->bqhd', p, jnp.concatenate([vc, v_strip], 1))

    o = lax.map(row_step, (r_idx, row_start))
    out = o.transpose(1, 0, 2, 3, 4).reshape(b, s, NA_HEADS * NA_HEAD_DIM) @ w_o
    out_c = None
    if need_ctx:
        out_c = _block_attention(qc[:, :, :, None], kc, vc, scale) @ w_o
    return out, out_c

def _gqa_proj(t, w_qkv, q_norm, k_norm, rows, cols):
    bb, ss, _ = t.shape
    nq = GQA_Q_HEADS * GQA_HEAD_DIM
    nk = GQA_KV_HEADS * GQA_HEAD_DIM
    qkv = t @ w_qkv
    q = _rms_norm(qkv[..., :nq].reshape(bb, ss, GQA_Q_HEADS, GQA_HEAD_DIM), q_norm)
    k = _rms_norm(qkv[..., nq:nq + nk].reshape(bb, ss, GQA_KV_HEADS, GQA_HEAD_DIM), k_norm)
    v = qkv[..., nq + nk:].reshape(bb, ss, GQA_KV_HEADS, GQA_HEAD_DIM)
    if rows is not None:
        q = _rope_2d(q, rows, cols)
        k = _rope_2d(k, rows, cols)
    return q.reshape(bb, ss, GQA_KV_HEADS, GQA_GROUP, GQA_HEAD_DIM), k, v

def _gqa_mixer(h, hc, w_qkv, q_norm, k_norm, w_o, need_ctx):
    rows, cols = _grid_positions(h.shape[1])
    scale = GQA_HEAD_DIM ** -0.5
    q, k, v = _gqa_proj(h, w_qkv, q_norm, k_norm, rows, cols)
    qc, kc, vc = _gqa_proj(hc, w_qkv, q_norm, k_norm, None, None)
    out = _block_attention(q, jnp.concatenate([kc, k], 1), jnp.concatenate([vc, v], 1), scale) @ w_o
    out_c = None
    if need_ctx:
        out_c = _block_attention(qc, kc, vc, scale) @ w_o
    return out, out_c

def _mlp(h, w1, w2):
    return jnp.square(jax.nn.relu(h @ w1)) @ w2

def second_inputs(seed: int = 0) -> dict:
    key = jax.random.key(seed)
    ks = iter(jax.random.split(key, 32))
    beta = (8.0 * DEPTH_2) ** -0.25
    n_a = len(range(0, DEPTH_2, N_MIXERS))
    n_b = len(range(1, DEPTH_2, N_MIXERS))
    n_c = len(range(2, DEPTH_2, N_MIXERS))
    D = D_MODEL

    def nrm(shape, s=1.0):
        return jax.random.normal(next(ks), shape, jnp.float32) * s

    def w(shape, fan_in, g=1.0):
        return nrm(shape, g * fan_in ** -0.5)

    def gain(shape):
        return 1.0 + nrm(shape, 0.05)

    return {
        "x": nrm((BATCH, SEQ, D)),
        "c": nrm((BATCH, D)),
        "ctx": nrm((BATCH, CTX_LEN, D)),
        "c_ctx": nrm((D,)),
        "ada_w": w((DEPTH_2, D, 6 * D), D),
        "ada_b": nrm((DEPTH_2, 6 * D), 0.02),
        "ln1_g": gain((DEPTH_2, D)),
        "ln1_b": nrm((DEPTH_2, D), 0.02),
        "ln2_g": gain((DEPTH_2, D)),
        "ln2_b": nrm((DEPTH_2, D), 0.02),
        "mlp_w1": w((DEPTH_2, D, D_FF_2), D),
        "mlp_w2": w((DEPTH_2, D_FF_2, D), D_FF_2, beta),
        "mla_w_dq": w((n_a, D, MLA_Q_RANK), D),
        "mla_q_norm": gain((n_a, MLA_Q_RANK)),
        "mla_w_uq": w((n_a, MLA_Q_RANK, MLA_HEADS * (MLA_NOPE + MLA_ROPE)), MLA_Q_RANK),
        "mla_w_dkv": w((n_a, D, MLA_KV_RANK + MLA_ROPE), D),
        "mla_kv_norm": gain((n_a, MLA_KV_RANK)),
        "mla_w_ukv": w((n_a, MLA_KV_RANK, MLA_HEADS * (MLA_NOPE + MLA_V)), MLA_KV_RANK),
        "mla_w_o": w((n_a, MLA_HEADS * MLA_V, D), MLA_HEADS * MLA_V, beta),
        "na_w_qkv": w((n_b, D, 3 * NA_HEADS * NA_HEAD_DIM), D),
        "na_b_qkv": nrm((n_b, 3 * NA_HEADS * NA_HEAD_DIM), 0.02),
        "na_rpb": nrm((n_b, NA_HEADS, 2 * NA_WIN_ROWS - 1, 2 * NA_WIN_COLS - 1), 0.1),
        "na_w_o": w((n_b, NA_HEADS * NA_HEAD_DIM, D), NA_HEADS * NA_HEAD_DIM, beta),
        "gqa_w_qkv": w((n_c, D, (GQA_Q_HEADS + 2 * GQA_KV_HEADS) * GQA_HEAD_DIM), D),
        "gqa_q_norm": gain((n_c, GQA_HEAD_DIM)),
        "gqa_k_norm": gain((n_c, GQA_HEAD_DIM)),
        "gqa_w_o": w((n_c, GQA_Q_HEADS * GQA_HEAD_DIM, D), GQA_Q_HEADS * GQA_HEAD_DIM, beta),
    }

def second_block(x, c, ctx, c_ctx, ada_w, ada_b, ln1_g, ln1_b, ln2_g, ln2_b, mlp_w1, mlp_w2,
              mla_w_dq, mla_q_norm, mla_w_uq, mla_w_dkv, mla_kv_norm, mla_w_ukv, mla_w_o,
              na_w_qkv, na_b_qkv, na_rpb, na_w_o,
              gqa_w_qkv, gqa_q_norm, gqa_k_norm, gqa_w_o):
    alpha = (2.0 * DEPTH_2) ** 0.25
    for i in range(DEPTH_2):
        kind, j = i % N_MIXERS, i // N_MIXERS
        need_ctx = i < DEPTH_2 - 1
        mod = (jax.nn.silu(c) @ ada_w[i] + ada_b[i])[:, None, :]
        mod_c = jax.nn.silu(c_ctx) @ ada_w[i] + ada_b[i]
        sh1, sc1, g1, sh2, sc2, g2 = jnp.split(mod, 6, axis=-1)
        csh1, csc1, cg1, csh2, csc2, cg2 = jnp.split(mod_c, 6, axis=-1)

        h = x * (1 + sc1) + sh1
        hc = ctx * (1 + csc1) + csh1
        if kind == 0:
            y, yc = _mla_mixer(h, hc, mla_w_dq[j], mla_q_norm[j], mla_w_uq[j], mla_w_dkv[j],
                               mla_kv_norm[j], mla_w_ukv[j], mla_w_o[j], need_ctx)
        elif kind == 1:
            y, yc = _na_mixer(h, hc, na_w_qkv[j], na_b_qkv[j], na_rpb[j], na_w_o[j], need_ctx)
        else:
            y, yc = _gqa_mixer(h, hc, gqa_w_qkv[j], gqa_q_norm[j], gqa_k_norm[j], gqa_w_o[j], need_ctx)
        x = _layer_norm(alpha * x + g1 * y, ln1_g[i], ln1_b[i])
        if need_ctx:
            ctx = _layer_norm(alpha * ctx + cg1 * yc, ln1_g[i], ln1_b[i])

        x = _layer_norm(alpha * x + g2 * _mlp(x * (1 + sc2) + sh2, mlp_w1[i], mlp_w2[i]), ln2_g[i], ln2_b[i])
        if need_ctx:
            ctx = _layer_norm(alpha * ctx + cg2 * _mlp(ctx * (1 + csc2) + csh2, mlp_w1[i], mlp_w2[i]),
                              ln2_g[i], ln2_b[i])
    return x


def setup_inputs(seed=0):
    out = dict(first_inputs(seed))
    for name, value in second_inputs(seed + 1).items():
        if name != "x":
            out[name + "_2"] = value
    return out


def reference(
    x, norm1_g, w_in, lam_q1, lam_k1, lam_q2, lam_k2, subln_g, w_out, rel_bias, norm2_g,
    w_router, w_gate, w_up, w_down, norm_f_g, c_2, ctx_2, c_ctx_2, ada_w_2, ada_b_2, ln1_g_2,
    ln1_b_2, ln2_g_2, ln2_b_2, mlp_w1_2, mlp_w2_2, mla_w_dq_2, mla_q_norm_2, mla_w_uq_2,
    mla_w_dkv_2, mla_kv_norm_2, mla_w_ukv_2, mla_w_o_2, na_w_qkv_2, na_b_qkv_2, na_rpb_2,
    na_w_o_2, gqa_w_qkv_2, gqa_q_norm_2, gqa_k_norm_2, gqa_w_o_2,
):
    x = first_block(
        x, norm1_g, w_in, lam_q1, lam_k1, lam_q2, lam_k2, subln_g, w_out, rel_bias, norm2_g,
        w_router, w_gate, w_up, w_down, norm_f_g,
    )
    return second_block(
        x, c_2, ctx_2, c_ctx_2, ada_w_2, ada_b_2, ln1_g_2, ln1_b_2, ln2_g_2, ln2_b_2, mlp_w1_2,
        mlp_w2_2, mla_w_dq_2, mla_q_norm_2, mla_w_uq_2, mla_w_dkv_2, mla_kv_norm_2, mla_w_ukv_2,
        mla_w_o_2, na_w_qkv_2, na_b_qkv_2, na_rpb_2, na_w_o_2, gqa_w_qkv_2, gqa_q_norm_2,
        gqa_k_norm_2, gqa_w_o_2,
    )


_drawn_inputs = setup_inputs


def setup_inputs(seed=0):
    import zlib

    import numpy as np

    out = dict(_drawn_inputs(seed))
    spreads = {}
    factors = {'lam_q1': 3.134,
     'lam_q2': 8.0,
     'subln_g': 4.225,
     'norm2_g': 3.586,
     'norm_f_g': 2.85,
     'mla_q_norm_2': 8.0,
     'mla_kv_norm_2': 8.0,
     'na_b_qkv_2': 8.0,
     'na_rpb_2': 8.0}
    for name, (base, spread) in spreads.items():
        noise = np.random.default_rng([zlib.crc32(name.encode()), seed]).standard_normal(out[name].shape)
        drawn = base * np.exp(spread * noise) if base else spread * noise
        out[name] = __import__('jax').numpy.asarray(drawn.astype(out[name].dtype))
    for name, factor in factors.items():
        out[name] = (out[name] * factor).astype(out[name].dtype)
    return out
```

```python
from contextlib import ExitStack

import numpy as np

import concourse.bass as bass
from concourse import mybir

F32 = mybir.dt.float32
ALU = mybir.AluOpType
ACT = mybir.ActivationFunctionType
AX = mybir.AxisListType

P = 128
D = 1024
KC = D // P
S = 256
NT = S // P
HD = 64
DIFF_HEADS, DIL_HEADS = 4, 8
HALF_W = D // 2
N_IN = 3 * D
N_EXPERTS = 16
CAP = 2 * S // N_EXPERTS
D_FF = 2816
FCH = D_FF // P
D_FF2 = 4096
MLA_HEADS, Q_RANK, KV_RANK, NOPE, ROPE = 8, 512, 256, 128, 64
NA_HEADS, NA_ROWS, NA_COLS, GRID_W = 16, 8, 16, 64
RPB_W = 2 * NA_COLS - 1
RPB_N = (2 * NA_ROWS - 1) * RPB_W
MLA_SCALE = float(NOPE + ROPE) ** -0.5
ALPHA = 4.0 ** 0.25
NEG = -1e30
SLOTS, SLOT = 8, 3072
REL = 2 * S - 1
WIN = 3 * P
NA_WIN = 5 * RPB_W + GRID_W

C_ID, C_FLIP, C_MASK, C_ROPE, C_IOTA, C_ALL = 0, 128, 256, 512, 768, 800
V_ADA, V_N1, V_N2, V_C, V_SUB, V_QN, V_KVN, V_BQKV, V_ALL = 0, 96, 104, 112, 128, 129, 133, 135, 159


def shape_constants():
    cst = np.zeros((P, C_ALL), np.float32)
    cst[:, C_ID:C_ID + P] = np.eye(P)
    cst[:, C_FLIP:C_FLIP + P] = np.eye(P)[::-1]
    c = np.arange(GRID_W)
    start = np.clip(c - NA_COLS // 2, 0, GRID_W - NA_COLS)
    valid = (c[None, :] >= start[:, None]) & (c[None, :] < start[:, None] + NA_COLS)
    cst[:, C_MASK:C_MASK + 256] = np.tile(np.where(valid, 0.0, NEG), (2, 4))
    freqs = np.float32(10000.0) ** (-np.arange(16, dtype=np.float32) / np.float32(16))
    t = np.arange(S)
    pos = np.stack([t // GRID_W, t % GRID_W], 1).astype(np.float32)
    ang = (pos[:, :, None] * freqs).reshape(NT, P, 32).transpose(1, 0, 2)
    for n, table in enumerate((np.cos(ang) * MLA_SCALE, np.sin(ang) * MLA_SCALE, np.cos(ang), np.sin(ang))):
        cst[:, C_ROPE + 64 * n:C_ROPE + 64 * n + 64] = table.reshape(P, 64)
    cst[:, C_IOTA:C_IOTA + CAP] = np.arange(CAP)
    rel = np.arange(REL) - (S - 1)
    n = np.abs(rel)
    large = 8 + (np.log(np.maximum(n, 1).astype(np.float32) / np.float32(8)) / np.float32(np.log(128.0)) * 8).astype(np.int32)
    bucket = np.where(rel > 0, 16, 0) + np.where(n < 8, n, np.minimum(large, 15))
    hot = np.zeros((32, 512), np.float32)
    hot[bucket, np.arange(REL)] = 1.0
    many = (n <= 64).astype(int) + (n % 4 == 0) + (n % 16 == 0)
    table = np.zeros((12, 512), np.float32)
    table[DIFF_HEADS:, :REL] = np.where(many > 0, np.log(np.maximum(many, 1)), NEG)
    return {"cst": cst, "bucket_hot": hot, "pattern_log": table}


class Steps:

    def __init__(self, sem, names):
        self.sem, self.names, self.done = sem, list(names), 0

    def __call__(self, name):
        assert self.names[self.done] == name, (self.names[self.done], name)
        self.done += 1
        return 1

    def at(self, name):
        return self.names.index(name) + 1


class Count:

    def __init__(self, sem):
        self.sem, self.n = sem, 0

    def take(self, k):
        self.n += k
        return self.n - k


class Job:

    def __init__(self, mms, evac, on, last_of=()):
        self.mms, self.evac, self.on, self.last_of = mms, evac, on, last_of


def build(nc, A):
    ctx = ExitStack()
    with ctx:
        def sem(name):
            return ctx.enter_context(nc.semaphore(name))

        def sb(name, shape, on=None):
            return (on or ctx).enter_context(nc.sbuf_tensor(name, [P] + list(shape), F32))

        ps = ctx.enter_context(nc.psum_tensor("ps", [P, 8, 512], F32))
        ring = sb("ring", [SLOTS, SLOT])
        cst = sb("cst", [C_ALL])
        vcol = sb("vcol", [160])
        x = sb("x", [NT, D])
        modc = sb("modc", [2, 48, 2])
        small = sb("small", [64])
        zeros = sb("zeros", [512])
        e_own = sem("moe_own")
        scp = sb("scp", [KC, 32])
        ident = cst[:, C_ID:C_ID + P]
        flip = cst[:, C_FLIP:C_FLIP + P]

        slot_loaded = [sem(f"slot{i}_loaded") for i in range(SLOTS)]
        job_done = Count(sem("job_done"))
        job_act = Count(sem("job_act_evac"))
        job_dve = Count(sem("job_dve_evac"))
        score_done = Count(sem("score_done"))
        max_done = Count(sem("max_done"))
        exp_done = Count(sem("exp_done"))
        probT_done = Count(sem("probT_done"))
        probT_sb = Count(sem("probT_sb"))
        pv_done = Count(sem("pv_done"))
        out_done = Count(sem("out_done"))
        ada_done = Count(sem("ada_done"))
        mlp_used = Count(sem("mlp_piece_used"))
        relu_done = Count(sem("relu_done"))
        square_done = Count(sem("square_done"))

        pieces = []
        released = {}
        loads = [0] * SLOTS
        arrival = {}
        fed = [0]

        def plan(src, cols):
            n = len(pieces)
            pieces.append((src, cols))
            loads[n % SLOTS] += 1
            arrival[n] = 16 * loads[n % SLOTS]
            return n

        def plan_loop(first, total):
            ids = [plan(*f) for f in first]
            for _ in range(total - len(first)):
                n = len(pieces)
                pieces.append(None)
                loads[n % SLOTS] += 1
                arrival[n] = 16 * loads[n % SLOTS]
            return ids[0]

        def slot(n, cols):
            return ring[:, n % SLOTS, 0:cols]

        def feed(sp, limit=None):
            while fed[0] < len(pieces) and (limit is None or fed[0] < limit):
                n = fed[0]
                if pieces[n] is None or (n >= SLOTS and n - SLOTS not in released):
                    return
                if n >= SLOTS:
                    sp.wait_ge(*released[n - SLOTS])
                src, cols = pieces[n]
                dst = slot(n, cols)
                if len(src.shape) == 3:
                    dst = dst.rearrange("p (k f) -> p k f", k=src.shape[1])
                sp.dma_start(dst, src).then_inc(slot_loaded[n % SLOTS], 16)
                fed[0] += 1

        def arrived(pe, n):
            pe.wait_ge(slot_loaded[n % SLOTS], arrival[n])

        class Run:
            def __init__(self, jobs, banks=(0, 1, 2, 3)):
                self.jobs, self.banks = jobs, banks
                self.base = job_done.take(len(jobs))
                self.pos, self.count = [], {"act": 0, "dve": 0}
                self.first = {"act": job_act.take(sum(j.on == "act" for j in jobs)),
                              "dve": job_dve.take(sum(j.on == "dve" for j in jobs))}
                for j in jobs:
                    self.count[j.on] += 1
                    self.pos.append(self.count[j.on])

            def out_of(self, eng, i):
                j = self.jobs[i]
                s = job_act if j.on == "act" else job_dve
                eng.wait_ge(s.sem, self.first[j.on] + self.pos[i])

            def finished(self, eng):
                for on, s in (("act", job_act), ("dve", job_dve)):
                    if self.count[on]:
                        eng.wait_ge(s.sem, self.first[on] + self.count[on])

            def pe(self, pe):
                seen = set()
                for i, j in enumerate(self.jobs):
                    if i >= len(self.banks):
                        self.out_of(pe, i - len(self.banks))
                    bank = ps[:, self.banks[i % len(self.banks)], :]
                    for (rows, lo, hi), lhsT, rhs, start, stop, tr, piece in j.mms:
                        if piece is not None and piece not in seen:
                            arrived(pe, piece)
                            seen.add(piece)
                        if tr:
                            last = nc.tensor.transpose(bank[0:rows, lo:hi], lhsT, rhs)
                        else:
                            last = nc.tensor.matmul(bank[0:rows, lo:hi], lhsT, rhs, start=start, stop=stop)
                    last.then_inc(job_done.sem, 1)
                    for piece in j.last_of:
                        released[piece] = (job_done.sem, self.base + i + 1)

            def ev(self, eng, on):
                for i, j in enumerate(self.jobs):
                    if j.on == on:
                        eng.wait_ge(job_done.sem, self.base + i + 1)
                        s = job_act if on == "act" else job_dve
                        j.evac(ps[:, self.banks[i % len(self.banks)], :]).then_inc(s.sem, 1)

        def to_act(out, scale=1.0, bias=0.0, cols=None):
            return lambda bank: nc.scalar.activation(out, bank if cols is None else bank[:, 0:cols],
                                                     ACT.Identity, bias=bias, scale=scale)

        def to_dve(out, scale=None, bias=None, cols=None):
            def go(bank):
                b = bank if cols is None else bank[:, 0:cols]
                if scale is None and bias is None:
                    return nc.vector.tensor_copy(out, b)
                if bias is None:
                    return nc.vector.tensor_scalar(out, b, scale, None, ALU.mult)
                if scale is None:
                    return nc.vector.tensor_scalar(out, b, bias, None, ALU.add)
                return nc.vector.tensor_scalar(out, b, scale, bias, ALU.mult, ALU.add)
            return go

        def turn(i, out, scale=None, bias=None, cols=None):
            if i % 2 == 0:
                return to_act(out, 1.0 if scale is None else scale, 0.0 if bias is None else bias, cols), "act"
            return to_dve(out, scale, bias, cols), "dve"

        def transposes(n, src, dst, scale=None, bias=None):
            jobs = []
            for c in range(n):
                mms = [((P, t * P, t * P + P), src(t, c), ident, True, True, True, None) for t in range(NT)]
                ev, on = turn(c, dst(c), scale and scale(c), bias and bias(c), S)
                jobs.append(Job(mms, ev, on))
            return jobs

        def vc(i):
            return vcol[:, i:i + 1]

        class Attention:

            def __init__(self, name, units, probs, probsT, fill=None):
                self.units, self.probs, self.probsT, self.fill = units, probs, probsT, fill
                n = len(units)
                self.b = {k: c.take(n) for k, c in (("s", score_done), ("m", max_done), ("e", exp_done),
                                                    ("t", probT_done), ("ts", probT_sb), ("pv", pv_done),
                                                    ("o", out_done))}
                self.scaled = 0

            def finished(self, eng):
                eng.wait_ge(out_done.sem, self.b["o"] + len(self.units))

            def pe(self, pe):
                def scores(u):
                    if u >= 2:
                        pe.wait_ge(exp_done.sem, self.b["e"] + u - 1)
                    for lo, hi, lhsT, rhs, start, stop in self.units[u]["scores"]:
                        last = nc.tensor.matmul(ps[:, u % 2, lo:hi], lhsT, rhs, start=start, stop=stop,
                                                skip_group_check=True)
                    last.then_inc(score_done.sem, 1)

                scores(0)
                for u, unit in enumerate(self.units):
                    if u + 1 < len(self.units):
                        scores(u + 1)
                    if self.fill is not None:
                        self.fill(pe, u)
                    pe.wait_ge(exp_done.sem, self.b["e"] + u + 1)
                    if u >= 1:
                        pe.wait_ge(probT_sb.sem, self.b["ts"] + u)
                    nk = 4 // unit["nt"]
                    for t in range(unit["nt"]):
                        for c in range(nk):
                            col = (c * unit["nt"] + t) * P
                            last = nc.tensor.transpose(ps[:, 2, col:col + P],
                                                       self.probs[:, u % 2, (t * nk + c) * P:(t * nk + c + 1) * P], ident)
                    last.then_inc(probT_done.sem, 1)
                    pe.wait_ge(probT_sb.sem, self.b["ts"] + u + 1)
                    if u >= 2:
                        pe.wait_ge(out_done.sem, self.b["o"] + u - 1)
                    for t in range(unit["nt"]):
                        for c in range(nk):
                            col = (c * unit["nt"] + t) * P
                            v = unit["v"](c)
                            o = 256 * (u % 2) + t * P
                            last = nc.tensor.matmul(ps[:, 3, o:o + v.shape[1]], self.probsT[:, u % 2, col:col + P],
                                                    v, start=(c == 0), stop=(c == nk - 1))
                    last.then_inc(pv_done.sem, 1)

            def act(self, act):
                for u, unit in enumerate(self.units):
                    act.wait_ge(max_done.sem, self.b["m"] + u + 1)
                    if u >= 2:
                        act.wait_ge(probT_done.sem, self.b["t"] + u - 1)
                    if u >= 4:
                        act.wait_ge(out_done.sem, self.b["o"] + u - 3)
                    w = 512 // unit["nt"]
                    for t in range(unit["nt"]):
                        last = nc.scalar.activation(self.probs[:, u % 2, t * w:t * w + w], ps[:, u % 2, t * w:t * w + w],
                                                    ACT.Exp, bias=small[:, 2 * (u % 4) + t:2 * (u % 4) + t + 1],
                                                    accum_out=small[:, 8 + 2 * (u % 4) + t:9 + 2 * (u % 4) + t])
                    last.then_inc(exp_done.sem, 1)

            def dve(self, dve, own, tally):
                def top(u):
                    nt = self.units[u]["nt"]
                    dve.wait_ge(score_done.sem, self.b["s"] + u + 1)
                    if u >= 4:
                        dve.wait_ge(exp_done.sem, self.b["e"] + u - 3)
                    nc.vector.reduce_max(small[:, 2 * (u % 4):2 * (u % 4) + nt],
                                         ps[:, u % 2, :].rearrange("p (t k) -> p t k", t=nt), AX.X,
                                         negate=True).then_inc(max_done.sem, 1)

                top(0)
                for u, unit in enumerate(self.units):
                    if u + 1 < len(self.units):
                        top(u + 1)
                    nt = unit["nt"]
                    dve.wait_ge(probT_done.sem, self.b["t"] + u + 1)
                    if u >= 2:
                        dve.wait_ge(pv_done.sem, self.b["pv"] + u - 1)
                    nc.vector.tensor_copy(self.probsT[:, u % 2, :], ps[:, 2, :]).then_inc(probT_sb.sem, 1)
                    inv = small[:, 16 + 2 * (u % 2):16 + 2 * (u % 2) + nt]
                    sums = small[:, 8 + 2 * (u % 4):8 + 2 * (u % 4) + nt]
                    dve.wait_ge(exp_done.sem, self.b["e"] + u + 1)
                    if u >= 2:
                        dve.wait_ge(out_done.sem, self.b["o"] + u - 1)
                    nc.vector.reciprocal(inv, sums).then_inc(own, 1)
                    tally[0] += 1
                    dve.wait_ge(own, tally[0])
                    if unit.get("minus") is not None:
                        nc.vector.tensor_scalar(inv, inv, unit["minus"], None, ALU.mult).then_inc(own, 1)
                        tally[0] += 1
                        dve.wait_ge(own, tally[0])
                    dve.wait_ge(pv_done.sem, self.b["pv"] + u + 1)
                    for t in range(nt):
                        out = unit["out"](t)
                        o = 256 * (u % 2) + t * P
                        part = ps[:, 3, o:o + out.shape[1]]
                        if unit.get("minus") is not None:
                            dve.wait_ge(out_done.sem, self.b["o"] + u)
                            last = nc.vector.scalar_tensor_tensor(out, part, inv[:, t:t + 1], out, ALU.mult, ALU.add)
                        else:
                            last = nc.vector.tensor_scalar(out, part, inv[:, t:t + 1], None, ALU.mult)
                    last.then_inc(out_done.sem, 1)

        dve_own = sem("dve_own")
        dve_count = [0]

        def link(dve, ins):
            dve_count[0] += 1
            ins.then_inc(dve_own, 1)
            dve.wait_ge(dve_own, dve_count[0])

        def view(tile, a, b):
            return tile[:, :, :].rearrange("p k s -> p (k s)")[:, 0:a * b].rearrange("p (a b) -> p a b", a=a)

        def rms_names(n):
            return [f"sq{i}" for i in range(n)] + ["sd"]

        def rms_act(act, acts, dves, srcs, junk, at):
            for i, src in enumerate(srcs):
                nc.scalar.activation(junk[:, 0:src.shape[1]], src, ACT.Square,
                                     accum_out=small[:, at + i:at + i + 1]).then_inc(acts.sem, acts(f"sq{i}"))
                act.wait_ge(acts.sem, acts.at(f"sq{i}"))
            act.wait_ge(dves.sem, dves.at("var"))
            nc.scalar.activation(small[:, at:at + len(srcs)], small[:, at:at + len(srcs)], ACT.Sqrt)\
              .then_inc(acts.sem, acts("sd"))

        def rms_dve(dve, acts, dves, groups, at):
            n = sum(g[0] for g in groups)
            dve.wait_ge(acts.sem, acts.at(f"sq{n - 1}"))
            i = at
            for count, width, eps in groups:
                last = nc.vector.tensor_scalar(small[:, i:i + count], small[:, i:i + count], 1.0 / width, eps,
                                               ALU.mult, ALU.add)
                i += count
            last.then_inc(dves.sem, dves("var"))
            dve.wait_ge(acts.sem, acts.at("sd"))
            link(dve, nc.vector.reciprocal(small[:, at:at + n], small[:, at:at + n]))

        def ln_dve(dve, acts, dves, y, gain, shift, stats):
            for t in range(NT):
                for h in range(2):
                    link(dve, nc.vector.bn_stats(stats[:, t, 6 * h:6 * h + 6], y[:, t, 512 * h:512 * h + 512]))
                link(dve, nc.vector.bn_aggr(stats[:, t, 12:14], stats[:, t, 0:12]))
            var = stats[:, :, 13:14]
            nc.vector.tensor_scalar(small[:, 40:42], var.rearrange("p t o -> p (t o)"), 1e-5, None, ALU.add)\
              .then_inc(dves.sem, dves("ln_var"))
            dve.wait_ge(acts.sem, acts.at("ln_sd"))
            link(dve, nc.vector.reciprocal(small[:, 42:44], small[:, 42:44]))
            for t in range(NT):
                link(dve, nc.vector.tensor_scalar(y[:, t, :], y[:, t, :], stats[:, t, 12:13], small[:, 42 + t:43 + t],
                                                  ALU.subtract, ALU.mult))
                link(dve, nc.vector.tensor_tensor(y[:, t, :], y[:, t, :], gain, ALU.mult))
                link(dve, nc.vector.tensor_tensor(y[:, t, :], y[:, t, :], shift, ALU.add))

        def ln_act(act, acts, dves):
            act.wait_ge(dves.sem, dves.at("ln_var"))
            nc.scalar.activation(small[:, 42:44], small[:, 40:42], ACT.Sqrt).then_inc(acts.sem, acts("ln_sd"))

        ada_w = A["ada_w_2"]
        ada_ids = [[], []]

        def plan_ada(layer):
            for half in range(2):
                for k in range(KC):
                    ada_ids[layer].append(plan(ada_w[layer, k * P:(k + 1) * P, half * N_IN:(half + 1) * N_IN], N_IN))

        def ada_piece(pe, layer, i, base):
            n = ada_ids[layer][i]
            half, k = divmod(i, KC)
            arrived(pe, n)
            for b in range(6):
                j = b % 4
                last = nc.tensor.matmul(ps[32 * j:32 * j + 32, 4 + 2 * half + b // 4, :], scp[:, k, :],
                                        slot(n, N_IN)[:, 512 * b:512 * b + 512], start=(k == 0), stop=(k == KC - 1))
            last.then_inc(ada_done.sem, 1)
            released[n] = (ada_done.sem, base + i + 1)

        def ada_jobs(layer, rows):
            runs = []
            for half in range(2):
                for b, parts in ((0, 128), (1, 64)):
                    q = 2 * half + b
                    chunk = 24 * half + 16 * b
                    mms = [((P, P * c, P * c + parts), rows[0:parts, q, P * c:P * c + P], ident[0:parts, 0:parts],
                            True, True, True, None) for c in range(4)]

                    def ev(bank, chunk=chunk, nj=parts // 32):
                        src = bank.rearrange("p (c j s) -> p j c s", c=4, j=4)[:, 0:nj, :, 0:2]
                        dst = modc[:, layer, chunk:chunk + 4 * nj, :].rearrange("p (j c) s -> p j c s", c=4)
                        add = vcol[:, V_ADA + 48 * layer + chunk:V_ADA + 48 * layer + chunk + 4 * nj]\
                            .rearrange("p (j c o) -> p j c o", c=4, o=1).to_broadcast([P, nj, 4, 2])
                        return nc.vector.tensor_tensor(dst, src, add, ALU.add)
                    runs.append(Job(mms, ev, "dve"))
            return runs

        def mod(layer, which, c, stream):
            return modc[:, layer, which * KC + c, stream:stream + 1]

        w_in = A["w_in"]
        id_in = [plan(w_in[0, k * P:(k + 1) * P, :], N_IN) for k in range(KC)]
        plan_ada(0)
        w_out = A["w_out"].rearrange("l (k p) f -> l p k f", p=P)

        def plan_square(w):
            where = {}
            for lo, hi in ((0, 3), (3, 6), (6, 8)):
                n = plan(w[:, lo:hi, :], (hi - lo) * D)
                for k in range(lo, hi):
                    where[k] = (n, k - lo)
            return where

        id_out = plan_square(w_out[0])

        def sq_at(where, k, lo, hi):
            n, r = where[k]
            return slot(n, SLOT)[:, r * D + lo:r * D + hi]

        small_loaded = sem("small_loaded")
        x_loaded = sem("x_loaded")
        wr_loaded = sem("w_router_loaded")
        w_r = sb("w_r", [KC, N_EXPERTS])
        table_dram = nc.dram_tensor("bias_table", [12, 512], F32).ap()

        first = ExitStack()
        h = sb("h", [NT, D], first)
        hT = sb("hT", [KC, S], first)
        early = ExitStack()
        qkT = sb("qkT", [16, S], early)
        vv = sb("vv", [NT, D], early)
        window = sb("window", [12, WIN], early)
        probs = sb("probs", [2, 512], early)
        probsT = sb("probsT", [2, 512], early)
        vrow = sb("vrow", [2, P], early)
        hot = sb("hot", [512], early)
        rel_b = sb("rel_b", [12], early)
        plog = sb("plog", [512], early)
        lamv = sb("lamv", [4, HD], early)
        junk = sb("junk", [D], early)
        a1 = Steps(sem("p1_act"), ["silu"] + rms_names(NT) + ["lam"])
        v1 = Steps(sem("p1_dve"), ["cols", "var", "h0", "h1", "lamsum", "scp"])
        t1 = sem("p1_table_stored")
        win_loaded = sem("window_loaded")

        vjobs = [Job([((P, 0, P), vrow[:, 0, :], ident, True, True, True, None)], to_dve(vcol[:, 0:P], cols=P), "dve"),
                 Job([((P, 0, V_ALL - P), vrow[0:V_ALL - P, 1, :], ident[0:V_ALL - P, 0:V_ALL - P], True, True, True, None)],
                     to_dve(vcol[:, P:V_ALL], cols=V_ALL - P), "dve"),
                 Job([((12, 0, REL), rel_b[0:32, :], hot[0:32, 0:REL], True, True, False, None)],
                     lambda bank: nc.vector.tensor_tensor(plog[0:12, 0:REL], bank[0:12, 0:REL], plog[0:12, 0:REL], ALU.add),
                     "dve")]
        run_v = Run(vjobs)
        run_h = Run(transposes(KC, lambda t, c: h[:, t, c * P:(c + 1) * P], lambda c: hT[:, c, :],
                               scale=lambda c: vc(V_N1 + c)))

        def projections():
            jobs = []
            cols = [0, 512, 1536, 2048]
            for n in range(16):
                lo = cols[n // 4] + (n % 4) * P
                mms = [((P, 0, S), slot(id_in[k], N_IN)[:, lo:lo + P], hT[:, k, :], k == 0, k == KC - 1, False, id_in[k])
                       for k in range(KC)]
                ev, on = turn(n, qkT[:, n, :], HD ** -0.5 if n // 4 in (0, 2) else None, None, S)
                jobs.append(Job(mms, ev, on))
            for n, lo in enumerate((1024, 2560)):
                for t in range(NT):
                    mms = [((P, 0, 512), hT[:, k, t * P:(t + 1) * P], slot(id_in[k], N_IN)[:, lo:lo + 512],
                            k == 0, k == KC - 1, False, id_in[k]) for k in range(KC)]
                    ev, on = turn(t, vv[:, t, 512 * n:512 * n + 512])
                    jobs.append(Job(mms, ev, on, id_in if (n, t) == (1, 1) else ()))
            return jobs

        run_p = Run(projections(), (0, 1, 2, 3, 4, 5, 6, 7))

        x_dram = A["x"].rearrange("b (t p) d -> p (b t) d", p=P)
        with nc.Block(no_gpsimd_drain=True) as block:
            @block.tensor
            def _(pe):
                pe.wait_ge(small_loaded, 16 * 17)
                run_v.pe(pe)
                run_v.finished(pe)
                pe.wait_ge(v1.sem, v1.at("h1"))
                run_h.pe(pe)
                run_h.finished(pe)
                run_p.pe(pe)

            @block.sync
            def _(sp):
                sp.dma_start(x[:, :, :], x_dram).then_inc(x_loaded, 16)
                feed(sp)
                run_v.finished(sp)
                sp.dma_start(table_dram, plog[0:12, :]).then_inc(t1, 16)
                sp.wait_ge(t1, 16)
                src = bass.AP(tensor=table_dram.tensor, offset=table_dram.offset, ap=[[1, P], [512, 12], [1, WIN]])
                sp.dma_start(window[:, :, :], src).then_inc(win_loaded, 16)

            @block.scalar
            def _(act):
                def load(dst, src):
                    act.dma_start(dst, src).then_inc(small_loaded, 16)
                load(cst[:, :], A["cst"])
                rows = [("ada_b_2", V_ADA, 96), ("norm1_g", V_N1, 8), ("norm2_g", V_N2, 8), ("c_2", V_C, 8),
                        ("c_ctx_2", V_C + 8, 8), ("subln_g", V_SUB, 1), ("mla_q_norm_2", V_QN, 4),
                        ("mla_kv_norm_2", V_KVN, 2), ("na_b_qkv_2", V_BQKV, 24)]
                for name, at, n in rows:
                    a = A[name]
                    a = a.rearrange("(n f) -> n f", f=P) if len(a.shape) == 1 else a.rearrange("l (n f) -> (l n) f", f=P)
                    load(vrow[at % P:at % P + n, at // P, :], a)
                load(hot[0:32, :], A["bucket_hot"])
                act.dma_start(w_r[:, :, :], A["w_router"].rearrange("l (k p) e -> p (l k) e", p=P)).then_inc(wr_loaded, 16)
                load(plog[0:12, :], A["pattern_log"])
                load(rel_b[0:32, :], A["rel_bias"])
                for i, name in enumerate(("lam_q1", "lam_k1", "lam_q2", "lam_k2")):
                    load(lamv[:, i, :], A[name].partition_broadcast(P))
                act.wait_ge(x_loaded, 16)
                act.wait_ge(v1.sem, v1.at("cols"))
                nc.scalar.activation(small[:, 44:60], vcol[:, V_C:V_C + 16], ACT.Exp, scale=-1.0)\
                  .then_inc(a1.sem, a1("silu"))
                rms_act(act, a1, v1, [x[:, t, :] for t in range(NT)], junk, 0)
                act.wait_ge(v1.sem, v1.at("lamsum"))
                nc.scalar.activation(small[:, 4:6], small[:, 4:6], ACT.Exp).then_inc(a1.sem, a1("lam"))
                run_h.ev(act, "act")
                run_p.ev(act, "act")

            @block.vector
            def _(dve):
                run_v.ev(dve, "dve")
                run_v.finished(dve)
                nc.vector.memset(zeros[:, :], 0.0)
                nc.vector.memset(scp[:, :, :], 0.0).then_inc(v1.sem, v1("cols"))
                dve.wait_ge(x_loaded, 16)
                rms_dve(dve, a1, v1, [(NT, D, 1e-6)], 0)
                for t in range(NT):
                    nc.vector.tensor_scalar(h[:, t, :], x[:, t, :], small[:, t:t + 1], None, ALU.mult)\
                      .then_inc(v1.sem, v1(f"h{t}"))
                lam4 = lamv[:, :, :].rearrange("p (a b) d -> p a b d", a=2)
                link(dve, nc.vector.tensor_tensor(lam4[:, :, 0, :], lam4[:, :, 0, :], lam4[:, :, 1, :], ALU.mult))
                nc.vector.reduce_sum(small[:, 4:6], lam4[:, :, 0, :], AX.X).then_inc(v1.sem, v1("lamsum"))
                dve.wait_ge(a1.sem, a1.at("silu"))
                link(dve, nc.vector.tensor_scalar(small[:, 44:60], small[:, 44:60], 1.0, None, ALU.add))
                link(dve, nc.vector.reciprocal(small[:, 44:60], small[:, 44:60]))
                dve.wait_ge(v1.sem, v1.at("cols"))
                nc.vector.tensor_tensor(scp[:, :, 0:2], vcol[:, V_C:V_C + 16].rearrange("p (s k) -> p k s", s=2),
                                        small[:, 44:60].rearrange("p (s k) -> p k s", s=2), ALU.mult)\
                  .then_inc(v1.sem, v1("scp"))
                dve.wait_ge(a1.sem, a1.at("lam"))
                link(dve, nc.vector.tensor_tensor(small[:, 24:25], small[:, 5:6], small[:, 4:5], ALU.subtract))
                link(dve, nc.vector.tensor_scalar(small[:, 25:26], small[:, 24:25], -0.2, None, ALU.add))
                run_h.ev(dve, "dve")
                run_p.ev(dve, "dve")

        def unit1(q, k, hh, table, v, out, minus=None):
            lo = HD * (hh % 2)
            sc = []
            for t in range(NT):
                sc.append((t * S, t * S + S, qkT[lo:lo + HD, q, t * P:(t + 1) * P], qkT[lo:lo + HD, k, :], True, False))
                off = P * (1 - t)
                sc.append((t * S, t * S + S, flip, window[:, table, off:off + S], False, True))
            return {"nt": NT, "scores": sc, "v": v, "out": out, "minus": minus}

        mix = h
        units = []
        for hh in range(DIFF_HEADS):
            for s in range(2):
                units.append(unit1(hh, 4 + hh, s, hh, lambda c, hh=hh: vv[:, c, P * hh:P * hh + P],
                                   lambda t, hh=hh: mix[:, t, P * hh:P * hh + P],
                                   small[:, 25:26] if s else None))
        for hh in range(DIL_HEADS):
            units.append(unit1(8 + hh // 2, 12 + hh // 2, hh, DIFF_HEADS + hh,
                               lambda c, hh=hh: vv[:, c, 512 + HD * hh:512 + HD * hh + HD],
                               lambda t, hh=hh: mix[:, t, 512 + HD * hh:512 + HD * hh + HD]))
        ada_base = ada_done.take(16)
        att1 = Attention("a1", units, probs, probsT, fill=lambda pe, u: ada_piece(pe, 0, u, ada_base))
        with nc.Block(no_gpsimd_drain=True) as block:
            @block.tensor
            def _(pe):
                pe.wait_ge(win_loaded, 16)
                att1.pe(pe)

            @block.sync
            def _(sp):
                feed(sp)

            @block.scalar
            def _(act):
                att1.act(act)

            @block.vector
            def _(dve):
                att1.dve(dve, dve_own, dve_count)
        early.close()

        gate_d = A["w_gate"].rearrange("l e k f -> (l e k) f")
        up_d = A["w_up"].rearrange("l e k f -> (l e k) f")
        down_d = A["w_down"].rearrange("l e k f -> (l e k) f")
        PIECES = 24

        def moe_piece(e, i):
            if i < 2 * KC:
                src = (gate_d, up_d)[i % 2]
                return src[bass.ds(e * D + (i // 2) * P, P), :], D_FF
            c = 3 * (i - 2 * KC)
            n = min(3, FCH - c)
            return down_d[bass.ds(e * D_FF + c * P, n * P), :].rearrange("(c p) f -> p c f", p=P), n * D

        moe0 = plan_loop([moe_piece(0, i) for i in range(SLOTS)], PIECES * N_EXPERTS)

        keep = ExitStack()
        xeT = sb("xeT", [KC, N_EXPERTS * CAP], keep)
        gT = sb("gT", [N_EXPERTS, S], keep)
        mid = ExitStack()
        rows0 = sb("rows0", [4, 512], mid)
        sq = sb("sq", [NT, 512], mid)
        sel = sb("sel", [NT, N_EXPERTS, CAP], mid)
        selg = sb("selg", [NT, N_EXPERTS, 4, CAP], mid)
        lg = sb("lg", [NT, 16], mid)
        aff = sb("aff", [NT, 16], mid)
        affT = sb("affT", [S], mid)
        work = sb("work", [S], mid)
        maskT = sb("maskT", [S], mid)
        top8 = sb("top8", [8], mid)
        slotT = sb("slotT", [NT, 16], mid)
        junk = sb("junk2", [D], mid)
        scol = sb("scol", [8], mid)
        a2 = Steps(sem("p2_act"), ["row0", "row2", "subsd"] + rms_names(NT) + ["ra"])
        v2 = Steps(sem("p2_dve"), ["row1", "row3", "subvar", "sub", "var", "h", "lmax", "aff", "slot", "sel"])

        def row_out(q, rows, parts, eng):
            out, src = rows[0:parts, q, :], ps[0:parts, 4 + q, :]
            return nc.scalar.activation(out, src, ACT.Identity) if eng == "act" else nc.vector.tensor_copy(out, src)

        run_ada = Run(ada_jobs(0, rows0))
        run_m = Run(transposes(KC, lambda t, c: mix[:, t, c * P:(c + 1) * P], lambda c: hT[:, c, :],
                               scale=lambda c: scol[:, c:c + 1]))

        def out_jobs():
            jobs = []
            for t in range(NT):
                for half in range(2):
                    mms = [((P, 0, 512), hT[:, k, t * P:(t + 1) * P], sq_at(id_out, k, 512 * half, 512 * half + 512),
                            k == 0, k == KC - 1, False, id_out[k][0]) for k in range(KC)]
                    part = x[:, t, 512 * half:512 * half + 512]
                    jobs.append(Job(mms, lambda bank, part=part: nc.vector.tensor_tensor(part, bank, part, ALU.add),
                                    "dve", [id_out[k][0] for k in (0, 3, 6)] if (t, half) == (1, 1) else ()))
            return jobs

        run_o = Run(out_jobs(), (4, 5, 6, 7))
        run_h2 = Run(transposes(KC, lambda t, c: h[:, t, c * P:(c + 1) * P], lambda c: hT[:, c, :],
                                scale=lambda c: vc(V_N2 + c)))
        run_r = Run([Job([((P, t * 16, t * 16 + 16), hT[:, k, t * P:(t + 1) * P], w_r[:, k, :], k == 0, k == KC - 1,
                           False, None) for t in range(NT) for k in range(KC)],
                         lambda bank: nc.vector.tensor_copy(lg[:, :, :].rearrange("p t e -> p (t e)"), bank[:, 0:32]), "dve")])
        run_at = Run([Job([((16, t * P, t * P + P), aff[:, t, :], ident, True, True, True, None) for t in range(NT)],
                          lambda bank: nc.vector.tensor_copy(affT[0:16, :], bank[0:16, 0:S]), "dve")])
        run_st = Run([Job([((P, t * 16, t * 16 + 16), work[0:16, t * P:(t + 1) * P], ident[0:16, 0:16], True, True, True, None)
                           for t in range(NT)],
                          lambda bank: nc.vector.tensor_copy(slotT[:, :, :].rearrange("p t e -> p (t e)"), bank[:, 0:32]),
                          "dve")])

        def gather_jobs():
            jobs = []
            for c in range(KC):
                mms = [((P, 0, 512), h[:, t, c * P:(c + 1) * P], sel[:, t, :, :].rearrange("p e s -> p (e s)"),
                        t == 0, t == NT - 1, False, None) for t in range(NT)]
                ev, on = turn(c, xeT[:, c, :], vc(V_N2 + c))
                jobs.append(Job(mms, ev, on))
            for e in range(0, N_EXPERTS, 2):
                mms = [((P, 256 * d + t * P, 256 * d + t * P + P), selg[:, t, e + d, :, :].rearrange("p j s -> p (j s)"),
                        ident, True, True, True, None) for d in range(2) for t in range(NT)]
                ev, on = turn(e // 2, gT[:, e:e + 2, :].rearrange("p e s -> p (e s)"))
                jobs.append(Job(mms, ev, on))
            return jobs

        run_g = Run(gather_jobs(), (0, 1, 2, 3, 4, 5, 6, 7))

        with nc.Block(no_gpsimd_drain=True) as block:
            @block.tensor
            def _(pe):
                pe.wait_ge(a2.sem, a2.at("row2"))
                pe.wait_ge(v2.sem, v2.at("row3"))
                run_ada.pe(pe)
                run_ada.finished(pe)
                pe.wait_ge(v2.sem, v2.at("sub"))
                run_m.pe(pe)
                run_m.finished(pe)
                run_o.pe(pe)
                pe.wait_ge(v2.sem, v2.at("h"))
                run_h2.pe(pe)
                run_h2.finished(pe)
                pe.wait_ge(wr_loaded, 16)
                run_r.pe(pe)
                pe.wait_ge(v2.sem, v2.at("aff"))
                run_at.pe(pe)
                pe.wait_ge(v2.sem, v2.at("slot"))
                run_st.pe(pe)
                pe.wait_ge(v2.sem, v2.at("sel"))
                run_g.pe(pe)

            @block.sync
            def _(sp):
                feed(sp)

            @block.scalar
            def _(act):
                row_out(0, rows0, 128, "act").then_inc(a2.sem, a2("row0"))
                row_out(2, rows0, 128, "act").then_inc(a2.sem, a2("row2"))
                act.wait_ge(v2.sem, v2.at("subvar"))
                nc.scalar.activation(small[:, 32:40], small[:, 24:32], ACT.Sqrt).then_inc(a2.sem, a2("subsd"))
                run_m.ev(act, "act")
                run_o.finished(act)
                rms_act(act, a2, v2, [x[:, t, :] for t in range(NT)], junk, 0)
                run_h2.ev(act, "act")
                act.wait_ge(v2.sem, v2.at("lmax"))
                for t in range(NT):
                    last = nc.scalar.activation(aff[:, t, :], lg[:, t, :], ACT.Exp, bias=small[:, 50 + t:51 + t],
                                                accum_out=small[:, 52 + t:53 + t])
                last.then_inc(a2.sem, a2("ra"))
                run_g.ev(act, "act")

            @block.vector
            def _(dve):
                row_out(1, rows0, 64, "dve").then_inc(v2.sem, v2("row1"))
                row_out(3, rows0, 64, "dve").then_inc(v2.sem, v2("row3"))
                link(dve, nc.vector.tensor_tensor(sq[:, :, :], mix[:, :, 0:512], mix[:, :, 0:512], ALU.mult))
                link(dve, nc.vector.reduce_sum(small[:, 24:32], sq[:, :, :].rearrange("p t (h f) -> p (t h) f", f=P), AX.X))
                nc.vector.tensor_scalar(small[:, 24:32], small[:, 24:32], 1.0 / P, 1e-5, ALU.mult, ALU.add)\
                  .then_inc(v2.sem, v2("subvar"))
                nc.vector.memset(scol[:, 4:8], 1.0)
                nc.vector.tensor_scalar(scol[:, 0:4], vc(V_SUB).to_broadcast([P, 4]), 1.0 - 0.2, None, ALU.mult)
                dve.wait_ge(a2.sem, a2.at("subsd"))
                link(dve, nc.vector.reciprocal(small[:, 32:40], small[:, 32:40]))
                for t in range(NT):
                    heads = mix[:, t, 0:512].rearrange("p (h f) -> p h f", f=P)
                    inv = small[:, 32 + 4 * t:36 + 4 * t].rearrange("p (h o) -> p h o", o=1).to_broadcast([P, 4, P])
                    last = nc.vector.tensor_tensor(heads, heads, inv, ALU.mult)
                last.then_inc(v2.sem, v2("sub"))
                run_ada.ev(dve, "dve")
                run_ada.finished(dve)
                for i in (1, 4):
                    part = modc[:, 0, 8 * i:8 * i + 8, :]
                    link(dve, nc.vector.tensor_scalar(part, part, 1.0, None, ALU.add))
                run_m.ev(dve, "dve")
                run_o.ev(dve, "dve")
                run_o.finished(dve)
                rms_dve(dve, a2, v2, [(NT, D, 1e-6)], 0)
                for t in range(NT):
                    last = nc.vector.tensor_scalar(h[:, t, :], x[:, t, :], small[:, t:t + 1], None, ALU.mult)
                last.then_inc(v2.sem, v2("h"))
                run_h2.ev(dve, "dve")
                run_r.ev(dve, "dve")
                run_r.finished(dve)
                nc.vector.reduce_max(small[:, 50:52], lg[:, :, :], AX.X, negate=True).then_inc(v2.sem, v2("lmax"))
                dve.wait_ge(a2.sem, a2.at("ra"))
                link(dve, nc.vector.reciprocal(small[:, 52:54], small[:, 52:54]))
                for t in range(NT):
                    last = nc.vector.tensor_scalar(aff[:, t, :], aff[:, t, :], small[:, 52 + t:53 + t], None, ALU.mult)
                last.then_inc(v2.sem, v2("aff"))
                run_at.ev(dve, "dve")
                run_at.finished(dve)
                src = affT
                for r in range(CAP // 8):
                    dst = work if r % 2 == 0 else maskT
                    link(dve, nc.vector.max(top8[0:16, :], src[0:16, :]))
                    link(dve, nc.vector.match_replace(dst[0:16, :], top8[0:16, :], src[0:16, :], -1.0))
                    src = dst
                link(dve, nc.vector.tensor_scalar(work[0:16, :], maskT[0:16, :], 0.0, None, ALU.is_lt))
                link(dve, nc.vector.tensor_tensor_scan(affT[0:16, :], work[0:16, :], work[0:16, :], 0.0, ALU.add, ALU.max))
                link(dve, nc.vector.tensor_tensor(affT[0:16, :], affT[0:16, :], work[0:16, :], ALU.mult))
                nc.vector.tensor_scalar(work[0:16, :], affT[0:16, :], -1.0, None, ALU.add).then_inc(v2.sem, v2("slot"))
                run_st.ev(dve, "dve")
                run_st.finished(dve)
                iota = cst[:, C_IOTA:C_IOTA + CAP].rearrange("p (o s) -> p o s", o=1).to_broadcast([P, N_EXPERTS, CAP])
                for t in range(NT):
                    slots = slotT[:, t, :].rearrange("p (e o) -> p e o", o=1).to_broadcast([P, N_EXPERTS, CAP])
                    last = nc.vector.tensor_tensor(sel[:, t, :, :], slots, iota, ALU.is_equal)
                link(dve, last)
                for t in range(NT):
                    s4 = sel[:, t, :, :].rearrange("p e (o s) -> p e o s", o=1).to_broadcast([P, N_EXPERTS, 4, CAP])
                    a4 = aff[:, t, :].rearrange("p (e o q) -> p e o q", o=1, q=1).to_broadcast([P, N_EXPERTS, 4, CAP])
                    last = nc.vector.tensor_tensor(selg[:, t, :, :, :], s4, a4, ALU.mult)
                last.then_inc(v2.sem, v2("sel"))
                run_g.ev(dve, "dve")
        mid.close()

        ex = ExitStack()
        xe = sb("xe", [KC, CAP], ex)
        gs = sb("gs", [S], ex)
        eg = sb("eg", [768], ex)
        hg = sb("hg", [768], ex)
        hgT = sb("hgT", [768], ex)
        ye = sb("ye", [D], ex)
        moe_used = sem("moe_piece_used")
        xe_ready, gs_ready = sem("xe_ready"), sem("gs_ready")
        e_exp, e_h, e_tr, e_trA, e_trV = (sem(f"moe_{n}") for n in ("exp", "h", "tr", "trA", "trV"))
        e_yA, e_yV, e_sc = sem("moe_yA"), sem("moe_yV"), sem("moe_scattered")
        first_slot = moe0 % SLOTS
        arr0 = [arrival[moe0 + i] for i in range(SLOTS)]

        with nc.Block(no_gpsimd_drain=True) as block:
            @block.tensor
            def _(pe):
                for b in range(4):
                    nc.tensor.matmul(ps[:, 4 + b, :], zeros[:, 0:P], zeros[:, :], start=True, stop=True)
                with pe.Fori(0, N_EXPERTS) as e:
                    def piece(i):
                        n = moe0 + i
                        pe.wait_ge(slot_loaded[n % SLOTS], e * (16 * PIECES // SLOTS) + (arr0[i % SLOTS] + 16 * (i // SLOTS)))
                        return slot(n, SLOT)
                    pe.wait_ge(xe_ready, e + 1)
                    pe.wait_ge(e_yA, e + 1)
                    pe.wait_ge(e_yV, e + 1)
                    pe.wait_ge(e_trV, e + 1)
                    for i in range(2 * KC):
                        k, up = divmod(i, 2)
                        w = piece(i)[:, 0:D_FF].rearrange("p (c f) -> p c f", f=P)
                        for j in range(4):
                            nc.tensor.matmul(ps[32 * j:32 * j + 32, up, :], xe[:, k, :], w[:, j:j + 13:4, :],
                                             start=(k == 0), stop=(k == KC - 1))
                        for j in range(4):
                            two = w[:, 16 + j:21 + j:4, :] if j < 2 else w[:, 16 + j:19 + j:2, :]
                            last = nc.tensor.matmul(ps[32 * j:32 * j + 32, 2, 256 * up:256 * up + 256], xe[:, k, :], two,
                                                    start=(k == 0 and not up), stop=(k == KC - 1), skip_group_check=True)
                        last.then_inc(moe_used, 1)
                    pe.wait_ge(e_h, e + 1)
                    pe.wait_ge(e_trA, e + 1)
                    for i in range(6):
                        n = P if i < 5 else 64
                        at = ps[:, 3, P * i:P * i + n] if i < 4 else ps[:, 0, P * (i - 4):P * (i - 4) + n]
                        last = nc.tensor.transpose(at, hg[0:n, P * i:P * i + P], cst[0:n, C_ID:C_ID + n])
                    last.then_inc(e_tr, 1)
                    pe.wait_ge(e_trA, e + 2)
                    pe.wait_ge(e_trV, e + 2)
                    for i in range(2 * KC, PIECES):
                        w = piece(i)
                        c0 = 3 * (i - 2 * KC)
                        for half in range(2):
                            for c in range(c0, min(c0 + 3, FCH)):
                                j = c % 4
                                last = nc.tensor.matmul(ps[32 * j:32 * j + 32, 1 + half, :],
                                                        hgT[:, P * (c // 4) + 32 * j:P * (c // 4) + 32 * j + 32],
                                                        w[:, (c - c0) * D + 512 * half:(c - c0) * D + 512 * half + 512],
                                                        start=(c < 4), stop=(c >= FCH - 4))
                        last.then_inc(moe_used, 1)
                    pe.wait_ge(gs_ready, e + 1)
                    pe.wait_ge(e_yA, e + 2)
                    pe.wait_ge(e_yV, e + 2)
                    for t in range(NT):
                        for half in range(2):
                            last = nc.tensor.matmul(ps[:, 4 + 2 * t + half, :], gs[:, t * P:(t + 1) * P],
                                                    ye[:, 512 * half:512 * half + 512], start=False, stop=True,
                                                    skip_group_check=True)
                    last.then_inc(e_sc, 1)
                for i in range(SLOTS):
                    released[moe0 + PIECES * N_EXPERTS - SLOTS + i] = (moe_used, PIECES * N_EXPERTS - SLOTS + i + 1)

            @block.sync
            def _(sp):
                def load(e, i, sub):
                    src, cols = moe_piece(e, i)
                    n = moe0 + i
                    dst = slot(n, cols)
                    if len(src.shape) == 3:
                        dst = dst.rearrange("p (k f) -> p k f", k=src.shape[1])
                    sp.wait_ge(moe_used, sub)
                    sp.dma_start(dst, src).then_inc(slot_loaded[n % SLOTS], 16)
                with sp.Fori(0, N_EXPERTS - 1) as e:
                    for i in range(SLOTS, PIECES):
                        load(e, i, e * PIECES + (i - SLOTS + 1))
                    for i in range(SLOTS):
                        load(e + 1, i, e * PIECES + (PIECES - SLOTS + i + 1))
                for i in range(SLOTS, PIECES):
                    load(N_EXPERTS - 1, i, (N_EXPERTS - 1) * PIECES + i - SLOTS + 1)
                fed[0] = moe0 + PIECES * N_EXPERTS
                feed(sp)

            @block.gpsimd
            def _(pool):
                with pool.Fori(0, N_EXPERTS) as e:
                    pool.wait_ge(e_sc, e + 1)
                    nc.gpsimd.tensor_copy(xe[:, :, :], xeT[:, :, bass.ds(e * CAP, CAP)]).then_inc(xe_ready, 1)
                    nc.gpsimd.tensor_copy(gs[:, :], gT[:, bass.ds(e, 1), :].rearrange("p o s -> p (o s)")).then_inc(gs_ready, 1)

            @block.scalar
            def _(act):
                nc.scalar.activation(eg[:, 0:1], zeros[:, 0:1], ACT.Identity).then_inc(e_yA, 1)
                nc.scalar.activation(eg[:, 1:2], zeros[:, 0:1], ACT.Identity).then_inc(e_trA, 1)
                nc.scalar.activation(eg[:, 2:3], zeros[:, 0:1], ACT.Identity).then_inc(e_sc, 1)
                with act.Fori(0, N_EXPERTS) as e:
                    act.wait_ge(moe_used, e * PIECES + 2 * KC)
                    nc.scalar.activation(eg[:, 0:512], ps[:, 0, :], ACT.Exp, scale=-1.0)
                    nc.scalar.activation(eg[:, 512:768], ps[:, 2, 0:256], ACT.Exp, scale=-1.0).then_inc(e_exp, 1)
                    act.wait_ge(e_tr, e + 1)
                    nc.scalar.activation(hgT[:, 0:512], ps[:, 3, :], ACT.Identity).then_inc(e_trA, 1)
                    act.wait_ge(moe_used, e * PIECES + PIECES)
                    nc.scalar.activation(ye[:, 0:512], ps[:, 1, :], ACT.Identity).then_inc(e_yA, 1)

            @block.vector
            def _(dve):
                nc.vector.memset(eg[:, 4:5], 0.0).then_inc(e_yV, 1)
                nc.vector.memset(eg[:, 5:6], 0.0).then_inc(e_trV, 1)
                with dve.Fori(0, N_EXPERTS) as e:
                    dve.wait_ge(e_exp, e + 1)
                    nc.vector.tensor_scalar(eg[:, :], eg[:, :], 1.0, None, ALU.add).then_inc(e_own, 1)
                    dve.wait_ge(e_own, e * 4 + 1)
                    nc.vector.reciprocal(eg[:, :], eg[:, :]).then_inc(e_own, 1)
                    dve.wait_ge(e_own, e * 4 + 2)
                    nc.vector.tensor_tensor(eg[:, 0:512], ps[:, 0, :], eg[:, 0:512], ALU.mult).then_inc(e_own, 1)
                    nc.vector.tensor_tensor(eg[:, 512:768], ps[:, 2, 0:256], eg[:, 512:768], ALU.mult).then_inc(e_own, 1)
                    dve.wait_ge(e_own, e * 4 + 4)
                    nc.vector.tensor_tensor(hg[:, 0:512], ps[:, 1, :], eg[:, 0:512], ALU.mult)
                    nc.vector.tensor_tensor(hg[:, 512:768], ps[:, 2, 256:512], eg[:, 512:768], ALU.mult).then_inc(e_h, 1)
                    dve.wait_ge(e_tr, e + 1)
                    nc.vector.tensor_copy(hgT[:, 512:704], ps[:, 0, 0:192]).then_inc(e_trV, 1)
                    dve.wait_ge(moe_used, e * PIECES + PIECES)
                    nc.vector.tensor_copy(ye[:, 512:1024], ps[:, 2, :]).then_inc(e_yV, 1)
        ex.close()
        keep.close()
        first.close()
        second = ExitStack()
        cx = sb("cx", [NT, D], second)
        kT = sb("kT", [KC, 2 * S], second)
        kpeT = sb("kpeT", [2 * S], second)
        va = sb("va", [2 * NT, D], second)
        gB = sb("gB", [D], second)
        lnb = sb("lnb", [2, D], second)
        stats = sb("stats", [NT, 14], second)
        cx_loaded = sem("ctx_loaded")
        ln_loaded = Count(sem("ln_loaded"))
        streams = (x, cx)

        af, vf = Steps(sem("pf_act"), rms_names(NT)), Steps(sem("pf_dve"), ["sum", "var"])
        with nc.Block(no_gpsimd_drain=True) as block:
            @block.scalar
            def _(act):
                act.dma_start(lnb[:, 0, :], A["norm_f_g"].partition_broadcast(P)).then_inc(ln_loaded.sem, 16)
                act.dma_start(cx[:, :, :], A["ctx_2"].rearrange("b (t p) d -> p (b t) d", p=P)).then_inc(cx_loaded, 16)
                act.wait_ge(vf.sem, vf.at("sum"))
                rms_act(act, af, vf, [x[:, t, :] for t in range(NT)], gB, 0)

            @block.sync
            def _(sp):
                feed(sp)

            @block.vector
            def _(dve):
                for t in range(NT):
                    last = nc.vector.tensor_tensor(x[:, t, :], ps[:, 4 + 2 * t:6 + 2 * t, :].rearrange("p b f -> p (b f)"),
                                                   x[:, t, :], ALU.add)
                last.then_inc(vf.sem, vf("sum"))
                rms_dve(dve, af, vf, [(NT, D, 1e-6)], 0)
                ln_loaded.take(16)
                dve.wait_ge(ln_loaded.sem, ln_loaded.n)
                for t in range(NT):
                    nc.vector.scalar_tensor_tensor(x[:, t, :], x[:, t, :], small[:, t:t + 1], lnb[:, 0, :], ALU.mult, ALU.mult)

        def modulated(layer, which, s, dst, off=0):
            y = streams[s]
            return transposes(KC, lambda t, c: y[:, t, c * P:(c + 1) * P], lambda c: dst[:, c, off:off + S],
                              scale=lambda c: mod(layer, which + 1, c, s), bias=lambda c: mod(layer, which, c, s))

        def gate_jobs(layer, which, s):
            jobs = []
            for half in range(2):
                mms = [((P, c * P, c * P + P), mod(layer, which, 4 * half + c, s).to_broadcast([P, P]), ident,
                        True, True, False, None) for c in range(4)]
                ev, on = turn(half, gB[:, 512 * half:512 * half + 512])
                jobs.append(Job(mms, ev, on))
            return jobs

        def load_ln(act, which, layer):
            for i, g in enumerate("gb"):
                act.dma_start(lnb[:, i, :], A[f"ln{which}_{g}_2"][layer:layer + 1, :].partition_broadcast(P)
                              .rearrange("q o d -> q (o d)")).then_inc(ln_loaded.sem, 16)
            ln_loaded.take(32)

        def gated(dve, bank, part, half):
            link(dve, nc.vector.tensor_tensor(bank, bank, gB[:, 512 * half:512 * half + 512], ALU.mult))
            return nc.vector.scalar_tensor_tensor(part, part, ALPHA, bank, ALU.mult, ALU.add)

        def square_jobs(dve, oT, where, s):
            jobs = []
            for t in range(NT):
                for half in range(2):
                    mms = [((P, 0, 512), oT[:, k, t * P:(t + 1) * P], sq_at(where, k, 512 * half, 512 * half + 512),
                            k == 0, k == KC - 1, False, where[k][0]) for k in range(KC)]
                    part = streams[s][:, t, 512 * half:512 * half + 512]
                    jobs.append(Job(mms, lambda bank, part=part, half=half: gated(nc.vector, bank, part, half), "dve",
                                    [where[k][0] for k in (0, 3, 6)] if (t, half) == (1, 1) else ()))
            return jobs

        def mixer_end(name, layer, s, o, oT, where, before=None):
            pre, act_pre, dve_pre, dve_post = before or ([], None, None, None)
            run_pre = Run(pre)
            run_gate = Run(gate_jobs(layer, 2, s), (4, 5))
            run_t = Run(transposes(KC, lambda t, c: o[:, t, c * P:(c + 1) * P], lambda c: oT[:, c, :]))
            run_w = Run(square_jobs(None, oT, where, s), (4, 5, 6, 7))
            a, v = Steps(sem(f"{name}_act"), ["pre", "ln_sd"]), Steps(sem(f"{name}_dve"), ["pre", "ln_var"])
            with nc.Block(no_gpsimd_drain=True) as block:
                @block.tensor
                def _(pe):
                    pe.wait_ge(a.sem, a.at("pre"))
                    pe.wait_ge(v.sem, v.at("pre"))
                    run_pre.pe(pe)
                    run_pre.finished(pe)
                    run_gate.pe(pe)
                    run_gate.finished(pe)
                    run_t.pe(pe)
                    run_t.finished(pe)
                    run_w.pe(pe)

                @block.sync
                def _(sp):
                    feed(sp)

                @block.scalar
                def _(act):
                    load_ln(act, 1, layer)
                    last = act_pre() if act_pre else nc.scalar.activation(small[:, 60:61], zeros[:, 0:1], ACT.Identity)
                    last.then_inc(a.sem, a("pre"))
                    run_gate.ev(act, "act")
                    run_t.ev(act, "act")
                    ln_act(act, a, v)

                @block.vector
                def _(dve):
                    last = dve_pre() if dve_pre else nc.vector.memset(small[:, 61:62], 0.0)
                    last.then_inc(v.sem, v("pre"))
                    run_pre.ev(dve, "dve")
                    run_pre.finished(dve)
                    if dve_post:
                        dve_post(dve)
                    run_gate.ev(dve, "dve")
                    run_t.ev(dve, "dve")
                    run_gate.finished(dve)
                    run_w.ev(dve, "dve")
                    run_w.finished(dve)
                    dve.wait_ge(ln_loaded.sem, ln_loaded.n)
                    ln_dve(dve, a, v, streams[s], lnb[:, 0, :], lnb[:, 1, :], stats)

        GROUPS = D_FF2 // (2 * P)
        TURN = 4
        ORDER = [(1, 0), (1, 1), (2, 0), (1, 2), (2, 1), (1, 3), (2, 2), (2, 3)]

        def mlp_piece(layer, m, i):
            w, g = ORDER[i]
            at = (TURN * m + g) * 2 * P
            if w == 1:
                return A["mlp_w1_2"][layer].rearrange("(k p) f -> p k f", p=P)[:, :, bass.ds(at, 2 * P)], KC * 2 * P
            return A["mlp_w2_2"][layer, bass.ds(at, 2 * P), :].rearrange("(k p) f -> p k f", p=P), 2 * D

        def plan_mlp(layer):
            return plan_loop([mlp_piece(layer, 0, i) for i in range(8)], 8 * GROUPS // TURN)

        def mlp(name, layer, s, n0):
            st = ExitStack()
            hT = sb(f"{name}_hT", [KC, S], st)
            relu = sb(f"{name}_relu", [2, 2 * S], st)
            h1 = sb(f"{name}_h1", [2, 2, S], st)
            run_gate = Run(gate_jobs(layer, 5, s), (4, 5))
            run_t = Run(modulated(layer, 3, s, hT))
            a, v = Steps(sem(f"{name}_act"), ["ln_sd"]), Steps(sem(f"{name}_dve"), ["sum", "ln_var"])
            used = mlp_used.take(8 * GROUPS // TURN)
            rb, qb = relu_done.take(GROUPS), square_done.take(GROUPS)
            turns = GROUPS // TURN
            arr = [arrival[n0 + i] for i in range(8)]
            pos = {wg: i + 1 for i, wg in enumerate(ORDER)}
            with nc.Block(no_gpsimd_drain=True) as block:
                @block.tensor
                def _(pe):
                    run_gate.pe(pe)
                    run_t.pe(pe)
                    run_gate.finished(pe)
                    run_t.finished(pe)
                    for b in range(4):
                        nc.tensor.matmul(ps[:, 4 + b, :], zeros[:, 0:P], zeros[:, :], start=True, stop=True)
                    with pe.Fori(0, turns) as m:
                        for i, (w, g) in enumerate(ORDER):
                            n = n0 + i
                            pe.wait_ge(slot_loaded[n % SLOTS], m * 16 + arr[i])
                            if w == 1:
                                w1 = slot(n, KC * 2 * P).rearrange("p (k f) -> p k f", k=KC)
                                for fc in range(2):
                                    for k in range(KC):
                                        last = nc.tensor.matmul(ps[:, g % 2, S * fc:S * fc + S],
                                                                w1[:, k, fc * P:(fc + 1) * P], hT[:, k, :],
                                                                start=(k == 0), stop=(k == KC - 1))
                            else:
                                pe.wait_ge(square_done.sem, m * TURN + (qb + g + 1))
                                w2 = slot(n, 2 * D).rearrange("p (k f) -> p k f", k=2)
                                for t in range(NT):
                                    for half in range(2):
                                        for fc in range(2):
                                            last = nc.tensor.matmul(ps[:, 4 + 2 * t + half, :],
                                                                    h1[:, g % 2, fc, t * P:(t + 1) * P],
                                                                    w2[:, fc, 512 * half:512 * half + 512],
                                                                    start=False, stop=True, skip_group_check=True)
                            last.then_inc(mlp_used.sem, 1)
                    for i in range(8):
                        released[n0 + 8 * turns - 8 + i] = (mlp_used.sem, used + 8 * turns - 8 + i + 1)

                @block.sync
                def _(sp):
                    with sp.Fori(0, turns - 1) as m:
                        for i in range(8):
                            src, cols = mlp_piece(layer, m + 1, i)
                            sp.wait_ge(mlp_used.sem, m * 8 + (used + i + 1))
                            sp.dma_start(slot(n0 + i, cols).rearrange("p (k f) -> p k f", k=src.shape[1]), src)\
                              .then_inc(slot_loaded[(n0 + i) % SLOTS], 16)
                    fed[0] = n0 + 8 * turns
                    feed(sp)

                @block.scalar
                def _(act):
                    load_ln(act, 2, layer)
                    run_gate.ev(act, "act")
                    run_t.ev(act, "act")
                    with act.Fori(0, turns) as m:
                        for g in range(TURN):
                            act.wait_ge(mlp_used.sem, m * 8 + (used + pos[1, g]))
                            nc.scalar.activation(relu[:, g % 2, :], ps[:, g % 2, :], ACT.Relu).then_inc(relu_done.sem, 1)
                    ln_act(act, a, v)

                @block.vector
                def _(dve):
                    run_gate.ev(dve, "dve")
                    run_t.ev(dve, "dve")
                    run_gate.finished(dve)
                    with dve.Fori(0, turns) as m:
                        for g in range(TURN):
                            dve.wait_ge(relu_done.sem, m * TURN + (rb + g + 1))
                            nc.vector.tensor_tensor(h1[:, g % 2, :, :].rearrange("p a b -> p (a b)"), relu[:, g % 2, :],
                                                    relu[:, g % 2, :], ALU.mult).then_inc(square_done.sem, 1)
                    dve.wait_ge(mlp_used.sem, used + 8 * turns)
                    for t in range(NT):
                        for half in range(2):
                            last = gated(dve, ps[:, 4 + 2 * t + half, :], streams[s][:, t, 512 * half:512 * half + 512], half)
                    last.then_inc(v.sem, v("sum"))
                    dve.wait_ge(v.sem, v.at("sum"))
                    dve.wait_ge(ln_loaded.sem, ln_loaded.n)
                    ln_dve(dve, a, v, streams[s], lnb[:, 0, :], lnb[:, 1, :], stats)
            st.close()

        def plan_mla(s):
            dq = A["mla_w_dq_2"].rearrange("l (k p) f -> p (l k) f", p=P)
            uq = A["mla_w_uq_2"].rearrange("l (k p) f -> p (l k) f", p=P)
            ids = {"dq": [plan(dq[:, 4 * i:4 * i + 4, :], 4 * Q_RANK) for i in range(2)],
                   "dkv": plan(A["mla_w_dkv_2"].rearrange("l (k p) f -> p (l k) f", p=P), KC * (KV_RANK + ROPE)),
                   "uq": [plan(uq[:, 2 * i:2 * i + 2, :], 2 * MLA_HEADS * (NOPE + ROPE)) for i in range(2)],
                   "ukv": [plan(A["mla_w_ukv_2"][0, k * P:(k + 1) * P, :], 2 * D) for k in range(2)]}
            if s == 1:
                plan_ada(1)
            ids["o"] = plan_square(A["mla_w_o_2"].rearrange("l (k p) f -> p (l k) f", p=P))
            return ids

        def mla(s, ids):
            name = f"mla{s}"
            st = ExitStack()
            hT = sb(f"{name}_hT", [KC, S], st)
            qT = sb(f"{name}_qT", [MLA_HEADS, S], st)
            cq = sb(f"{name}_cq", [NT, Q_RANK], st)
            ckv = sb(f"{name}_ckv", [NT, KV_RANK + ROPE], st)
            kpe = sb(f"{name}_kpe", [NT, 2 * ROPE], st)
            cqT = sb(f"{name}_cqT", [4, S], st)
            ckvT = sb(f"{name}_ckvT", [2, S], st)
            qpe = sb(f"{name}_qpe", [NT, 512], st)
            qpeT = sb(f"{name}_qpeT", [4, S], st)
            rot = view(cqT, 2, 512)
            off = S * (1 - s)
            voff = NT * (1 - s)

            run_t = Run(modulated(0, 0, s, hT))
            jobs = []
            for t in range(NT):
                mms = [((P, 0, Q_RANK), hT[:, k, t * P:(t + 1) * P],
                        slot(ids["dq"][k // 4], 4 * Q_RANK)[:, (k % 4) * Q_RANK:(k % 4 + 1) * Q_RANK],
                        k == 0, k == KC - 1, False, ids["dq"][k // 4]) for k in range(KC)]
                ev, on = turn(t, cq[:, t, :])
                jobs.append(Job(mms, ev, on, ids["dq"] if t else ()))
            w = KV_RANK + ROPE
            for t in range(NT):
                mms = [((P, 0, w), hT[:, k, t * P:(t + 1) * P], slot(ids["dkv"], KC * w)[:, k * w:(k + 1) * w],
                        k == 0, k == KC - 1, False, ids["dkv"]) for k in range(KC)]
                ev, on = turn(t, ckv[:, t, :], cols=w)
                jobs.append(Job(mms, ev, on, [ids["dkv"]] if t else ()))
            run_d = Run(jobs, (4, 5, 6, 7))
            run_c = Run(transposes(4, lambda t, c: cq[:, t, c * P:(c + 1) * P], lambda c: cqT[:, c, :],
                                   scale=lambda c: vc(V_QN + c))
                        + transposes(2, lambda t, c: ckv[:, t, c * P:(c + 1) * P], lambda c: ckvT[:, c, :],
                                     scale=lambda c: vc(V_KVN + c))
                        + transposes(1, lambda t, c: kpe[:, t, :], lambda c: kpeT[:, off:off + S]))

            def uq(k, lo, n, step=None):
                row = slot(ids["uq"][k // 2], 2 * 1536)[:, (k % 2) * 1536:(k % 2 + 1) * 1536]
                if step is None:
                    return row[:, lo:lo + n]
                return row.rearrange("p (h f) -> p h f", f=NOPE + ROPE)[:, :, NOPE:NOPE + ROPE]

            jobs = []
            for t in range(NT):
                mms = [((P, 0, 512), cqT[:, k, t * P:(t + 1) * P], uq(k, 0, 0, 1), k == 0, k == 3, False, ids["uq"][k // 2])
                       for k in range(4)]
                ev, on = turn(t, qpe[:, t, :], MLA_SCALE if s else None)
                jobs.append(Job(mms, ev, on))
            for hh in range(MLA_HEADS):
                mms = [((P, 0, S), uq(k, hh * (NOPE + ROPE), NOPE), cqT[:, k, :], k == 0, k == 3, False, ids["uq"][k // 2])
                       for k in range(4)]
                ev, on = turn(hh, qT[:, hh, :], MLA_SCALE, None, S)
                jobs.append(Job(mms, ev, on, ids["uq"] if hh == MLA_HEADS - 1 else ()))
            for hh in range(MLA_HEADS):
                mms = [((P, 0, S), slot(ids["ukv"][k], 2 * D)[:, 256 * hh:256 * hh + P], ckvT[:, k, :], k == 0, k == 1,
                        False, ids["ukv"][k]) for k in range(2)]
                ev, on = turn(hh, kT[:, hh, off:off + S], None, None, S)
                jobs.append(Job(mms, ev, on))
            for t in range(NT):
                for half in range(2):
                    def wv(k, half=half):
                        return slot(ids["ukv"][k], 2 * D).rearrange("p (h f) -> p h f", f=256)[:, 4 * half:4 * half + 4, P:256]
                    mms = [((P, 0, 512), ckvT[:, k, t * P:(t + 1) * P], wv(k), k == 0, k == 1, False, ids["ukv"][k])
                           for k in range(2)]
                    ev, on = turn(half, va[:, voff + t, 512 * half:512 * half + 512])
                    jobs.append(Job(mms, ev, on, ids["ukv"] if (t, half) == (1, 1) else ()))
            run_u = Run(jobs, (4, 5, 6, 7, 0, 1))
            run_q = Run(transposes(4, lambda t, c: qpe[:, t, c * P:(c + 1) * P], lambda c: qpeT[:, c, :]))

            def rope(dve, y, groups, table):
                v4 = y.rearrange("p (g a b f) -> p g a b f", g=groups, a=2, b=2)
                x1, x2 = (v4[:, :, :, b, :] for b in range(2))
                cs, sn = (cst[:, C_ROPE + 64 * (2 * table + n):][:, 0:64].rearrange("p (t a f) -> p t a f", t=2, a=2)
                          for n in range(2))
                def tab(z, t):
                    return z[:, t, :, :].rearrange("p (o a) f -> p o a f", o=1).to_broadcast([P, groups, 2, 16])
                n = groups * 32
                def r(i):
                    return rot[:, i // 2, (i % 2) * 256:(i % 2) * 256 + n].rearrange("p (g a f) -> p g a f", g=groups, a=2)
                def go(t):
                    for i, (z, w) in enumerate(((x1, cs), (x2, sn), (x1, sn), (x2, cs))):
                        last = nc.vector.tensor_tensor(r(i), z, tab(w, t), ALU.mult)
                    link(dve, last)
                    nc.vector.tensor_tensor(x1, r(0), r(1), ALU.subtract)
                    return nc.vector.tensor_tensor(x2, r(2), r(3), ALU.add)
                return go

            a = Steps(sem(f"{name}_act"), rms_names(4))
            v = Steps(sem(f"{name}_dve"), ["var", "norms", "rope_q"])
            o, oT, probs = view(hT, NT, D), qT, cq
            probsT = view(cqT, 2, 512)
            units = []
            nq = 1 if s == 0 else NT
            keys = 2 * S if s == 0 else S
            for hh in range(MLA_HEADS):
                for t0 in range(0, NT, nq):
                    sc = []
                    lo = HD * (hh % 2)
                    for t in range(nq):
                        tt = t0 + t
                        sc.append((t * keys, t * keys + keys, qT[:, hh, tt * P:(tt + 1) * P], kT[:, hh, 0:keys], True, False))
                        sc.append((t * keys, t * keys + keys, qpeT[lo:lo + HD, hh // 2, tt * P:(tt + 1) * P],
                                   kpeT[lo:lo + HD, 0:keys], False, True))
                    units.append({"nt": nq, "scores": sc, "v": lambda c, hh=hh: va[:, c, P * hh:P * hh + P],
                                  "out": lambda t, hh=hh, t0=t0: o[:, t0 + t, P * hh:P * hh + P]})
            fill = None
            if s == 1:
                base = ada_done.take(16)
                fill = lambda pe, u: [ada_piece(pe, 1, 2 * u + d, base) for d in range(2)]
            att = Attention(name, units, probs, probsT, fill=fill)

            with nc.Block(no_gpsimd_drain=True) as block:
                @block.tensor
                def _(pe):
                    if s == 1:
                        pe.wait_ge(cx_loaded, 16)
                    run_t.pe(pe)
                    run_t.finished(pe)
                    run_d.pe(pe)
                    pe.wait_ge(v.sem, v.at("norms"))
                    run_c.pe(pe)
                    run_c.finished(pe)
                    run_d.finished(pe)
                    run_u.pe(pe)
                    run_u.finished(pe)
                    if s == 0:
                        pe.wait_ge(v.sem, v.at("rope_q"))
                    run_q.pe(pe)
                    run_q.finished(pe)

                @block.sync
                def _(sp):
                    feed(sp)

                @block.scalar
                def _(act):
                    run_t.ev(act, "act")
                    run_d.ev(act, "act")
                    run_d.finished(act)
                    rms_act(act, a, v, [cq[:, 0, :], cq[:, 1, :], ckv[:, 0, 0:KV_RANK], ckv[:, 1, 0:KV_RANK]],
                            view(cqT, 1, 1024)[:, 0, :], 0)
                    run_c.ev(act, "act")
                    run_u.ev(act, "act")
                    run_q.ev(act, "act")

                @block.vector
                def _(dve):
                    run_t.ev(dve, "dve")
                    run_d.ev(dve, "dve")
                    run_d.finished(dve)
                    rms_dve(dve, a, v, [(NT, Q_RANK, 1e-6), (NT, KV_RANK, 1e-6)], 0)
                    for t in range(NT):
                        nc.vector.tensor_scalar(cq[:, t, :], cq[:, t, :], small[:, t:t + 1], None, ALU.mult)
                        nc.vector.tensor_scalar(ckv[:, t, 0:KV_RANK], ckv[:, t, 0:KV_RANK], small[:, 2 + t:3 + t],
                                                None, ALU.mult)
                        if s == 0:
                            link(dve, rope(dve, ckv[:, t, KV_RANK:], 1, 1)(t))
                        src = ckv[:, t, KV_RANK:].rearrange("p (o f) -> p o f", o=1).to_broadcast([P, 2, ROPE])
                        last = nc.vector.tensor_copy(kpe[:, t, :].rearrange("p (o f) -> p o f", o=2), src)
                    last.then_inc(v.sem, v("norms"))
                    run_c.ev(dve, "dve")
                    run_u.ev(dve, "dve")
                    run_u.finished(dve)
                    if s == 0:
                        for t in range(NT):
                            last = rope(dve, qpe[:, t, :], MLA_HEADS, 0)(t)
                            if t + 1 < NT:
                                link(dve, last)
                        last.then_inc(v.sem, v("rope_q"))
                    run_q.ev(dve, "dve")

            with nc.Block(no_gpsimd_drain=True) as block:
                @block.tensor
                def _(pe):
                    att.pe(pe)

                @block.sync
                def _(sp):
                    feed(sp)

                @block.scalar
                def _(act):
                    att.act(act)

                @block.vector
                def _(dve):
                    att.dve(dve, dve_own, dve_count)

            before = None
            if s == 1:
                rows1 = view(qT, 4, 512)

                def act_pre():
                    row_out(0, rows1, 128, "act")
                    return row_out(2, rows1, 128, "act")

                def dve_pre():
                    row_out(1, rows1, 64, "dve")
                    return row_out(3, rows1, 64, "dve")

                def dve_post(dve):
                    for i in (1, 4):
                        part = modc[:, 1, 8 * i:8 * i + 8, :]
                        link(dve, nc.vector.tensor_scalar(part, part, 1.0, None, ALU.add))
                before = (ada_jobs(1, rows1), act_pre, dve_pre, dve_post)
            mixer_end(f"{name}_end", 0, s, o, oT, ids["o"], before)
            st.close()

        ids_c = plan_mla(1)
        mlp_c = plan_mlp(0)
        ids_x = plan_mla(0)
        mlp_x = plan_mlp(0)
        w_qkv = A["na_w_qkv_2"]
        id_na = [plan(w_qkv[0, k * P:(k + 1) * P, :], N_IN) for k in range(KC)]
        id_nao = plan_square(A["na_w_o_2"].rearrange("l (k p) f -> p (l k) f", p=P))
        mlp_n = plan_mlp(1)

        mla(1, ids_c)
        mlp("mlp_c", 0, 1, mlp_c)
        mla(0, ids_x)
        mlp("mlp_x", 0, 0, mlp_x)

        st = ExitStack()
        hT2 = sb("na_hT", [KC, 2 * S], st)
        qT = sb("na_qT", [KC, S], st)
        vb = gB
        naw = sb("na_window", [NA_HEADS, NA_WIN], st)
        na_loaded = sem("na_loaded")
        run_tc = Run(modulated(1, 0, 1, hT2, 0) + modulated(1, 0, 0, hT2, S))
        jobs = []
        for n in range(KC):
            mms = [((P, 0, S), slot(id_na[k], N_IN)[:, n * P:(n + 1) * P], hT2[:, k, S:2 * S], k == 0, k == KC - 1, False,
                    id_na[k]) for k in range(KC)]

            def ev(bank, n=n):
                return nc.vector.tensor_scalar(qT[:, n, :], bank[:, 0:S], vc(V_BQKV + n), HD ** -0.5, ALU.add, ALU.mult)
            jobs.append(Job(mms, ev, "dve"))
        for n in range(KC):
            mms = [((P, 0, 2 * S), slot(id_na[k], N_IN)[:, D + n * P:D + (n + 1) * P], hT2[:, k, :], k == 0, k == KC - 1,
                    False, id_na[k]) for k in range(KC)]
            ev, on = turn(n, kT[:, n, :], None, vc(V_BQKV + KC + n))
            jobs.append(Job(mms, ev, on))
        for t in range(2 * NT):
            for half in range(2):
                mms = [((P, 0, 512), hT2[:, k, t * P:(t + 1) * P],
                        slot(id_na[k], N_IN)[:, 2 * D + 512 * half:2 * D + 512 * half + 512], k == 0, k == KC - 1, False,
                        id_na[k]) for k in range(KC)]

                def ev(bank, t=t, half=half):
                    return nc.vector.tensor_tensor(va[:, t, 512 * half:512 * half + 512], bank,
                                                   vb[:, 512 * half:512 * half + 512], ALU.add)
                jobs.append(Job(mms, ev, "dve", id_na if (t, half) == (3, 1) else ()))
        run_n = Run(jobs, (4, 5, 6, 7))
        with nc.Block(no_gpsimd_drain=True) as block:
            @block.tensor
            def _(pe):
                run_tc.pe(pe)
                run_tc.finished(pe)
                run_n.pe(pe)

            @block.sync
            def _(sp):
                feed(sp)

            @block.scalar
            def _(act):
                act.dma_start(vb[:, :], A["na_b_qkv_2"][0:1, 2 * D:3 * D].partition_broadcast(P)
                              .rearrange("q o d -> q (o d)")).then_inc(na_loaded, 16)
                rpb = A["na_rpb_2"]
                for par in range(2):
                    src = bass.AP(tensor=rpb.tensor, offset=rpb.offset + 4 * RPB_W + 15 + 31 * par - 63,
                                  ap=[[1, 64], [RPB_N, NA_HEADS], [1, NA_WIN]])
                    act.dma_start(naw[64 * par:64 * par + 64, :, :], src).then_inc(na_loaded, 16)
                run_tc.ev(act, "act")
                run_n.ev(act, "act")

            @block.vector
            def _(dve):
                run_tc.ev(dve, "dve")
                dve.wait_ge(na_loaded, 48)
                run_n.ev(dve, "dve")

        o = view(hT2, 4, D)[:, 0:NT, :]
        oT = view(hT2, 2 * KC, S)[:, KC:2 * KC, :]
        probs, probsT = (oT[:, 4 * i:4 * i + 4, :].rearrange("p k s -> p (k s)").rearrange("p (a b) -> p a b", a=2)
                         for i in range(2))
        units = []
        for hh in range(NA_HEADS):
            for t in range(NT):
                lo = HD * (hh % 2)
                win = naw[:, hh, RPB_W * (2 - 2 * t):RPB_W * (2 - 2 * t) + GRID_W]
                win = bass.AP(tensor=win.tensor, offset=win.offset, ap=[list(win.ap[0]), [RPB_W, 4], [1, GRID_W]])
                sc = [(0, 512, qT[lo:lo + HD, hh // 2, t * P:(t + 1) * P], kT[lo:lo + HD, hh // 2, :], True, False),
                      (S, 2 * S, flip, win, False, False),
                      (S, 2 * S, ident, cst[:, C_MASK:C_MASK + S], False, True)]
                units.append({"nt": 1, "scores": sc, "v": lambda c, hh=hh: va[:, c, HD * hh:HD * hh + HD],
                              "out": lambda q, hh=hh, t=t: o[:, t, HD * hh:HD * hh + HD]})
        att = Attention("na", units, probs, probsT)
        with nc.Block(no_gpsimd_drain=True) as block:
            @block.tensor
            def _(pe):
                att.pe(pe)

            @block.sync
            def _(sp):
                feed(sp)

            @block.scalar
            def _(act):
                att.act(act)

            @block.vector
            def _(dve):
                att.dve(dve, dve_own, dve_count)
        mixer_end("na_end", 1, 0, o, oT, id_nao)
        st.close()
        stored = sem("stored")
        mlp("mlp_n", 1, 0, mlp_n)
        with nc.Block(no_gpsimd_drain=True) as block:
            @block.sync
            def _(sp):
                sp.dma_start(A["out"].rearrange("b (t p) d -> p (b t) d", p=P), x[:, :, :]).then_inc(stored, 16)
                sp.wait_ge(stored, 16)
        second.close()


_INS = ["x", "norm1_g", "w_in", "lam_q1", "lam_k1", "lam_q2", "lam_k2", "subln_g", "w_out", "rel_bias", "norm2_g",
        "w_router", "w_gate", "w_up", "w_down", "norm_f_g", "c_2", "ctx_2", "c_ctx_2", "ada_w_2", "ada_b_2",
        "ln1_g_2", "ln1_b_2", "ln2_g_2", "ln2_b_2", "mlp_w1_2", "mlp_w2_2", "mla_w_dq_2", "mla_q_norm_2",
        "mla_w_uq_2", "mla_w_dkv_2", "mla_kv_norm_2", "mla_w_ukv_2", "mla_w_o_2", "na_w_qkv_2", "na_b_qkv_2",
        "na_rpb_2", "na_w_o_2"]


def kernel(**inputs):
    import concourse.bacc as bacc
    from concourse.bass_utils import run_bass_kernel_spmd

    nc = bacc.Bacc("TRN2", target_bir_lowering=False, num_devices=1)
    arrays, aps = {}, {}
    for name in _INS:
        arrays[f"in_{name}"] = np.ascontiguousarray(inputs[name])
    for name, table in shape_constants().items():
        arrays[f"in_{name}"] = table
    for name, a in arrays.items():
        aps[name[3:]] = nc.dram_tensor(name, a.shape, mybir.dt.from_np(a.dtype), kind="ExternalInput").ap()
    aps["out"] = nc.dram_tensor("out", (1, S, D), F32, kind="ExternalOutput").ap()
    build(nc, aps)
    r = run_bass_kernel_spmd(nc, [arrays], core_ids=[0])
    return r.results[0]["out"]
```

```python
from contextlib import ExitStack

import numpy as np

import concourse.bass as bass
from concourse import mybir

F32 = mybir.dt.float32
ALU = mybir.AluOpType
ACT = mybir.ActivationFunctionType
AX = mybir.AxisListType

P = 128
D = 1024
KC = D // P
S = 256
NT = S // P
HD = 64
DIFF_HEADS, DIL_HEADS = 4, 8
HALF_W = D // 2
N_IN = 3 * D
N_EXPERTS = 16
CAP = 2 * S // N_EXPERTS
D_FF = 2816
FCH = D_FF // P
D_FF2 = 4096
MLA_HEADS, Q_RANK, KV_RANK, NOPE, ROPE = 8, 512, 256, 128, 64
NA_HEADS, NA_ROWS, NA_COLS, GRID_W = 16, 8, 16, 64
RPB_W = 2 * NA_COLS - 1
RPB_N = (2 * NA_ROWS - 1) * RPB_W
MLA_SCALE = float(NOPE + ROPE) ** -0.5
ALPHA = 4.0 ** 0.25
NEG = -1e30
SLOTS, SLOT = 8, 3072
REL = 2 * S - 1
WIN = 3 * P
NA_WIN = 5 * RPB_W + GRID_W

C_ID, C_FLIP, C_MASK, C_ROPE, C_IOTA, C_ALL = 0, 128, 256, 512, 768, 800
V_ADA, V_N1, V_N2, V_C, V_SUB, V_QN, V_KVN, V_BQKV, V_ALL = 0, 96, 104, 112, 128, 129, 133, 135, 159


def shape_constants():
    cst = np.zeros((P, C_ALL), np.float32)
    cst[:, C_ID:C_ID + P] = np.eye(P)
    cst[:, C_FLIP:C_FLIP + P] = np.eye(P)[::-1]
    c = np.arange(GRID_W)
    start = np.clip(c - NA_COLS // 2, 0, GRID_W - NA_COLS)
    valid = (c[None, :] >= start[:, None]) & (c[None, :] < start[:, None] + NA_COLS)
    cst[:, C_MASK:C_MASK + 256] = np.tile(np.where(valid, 0.0, NEG), (2, 4))
    freqs = np.float32(10000.0) ** (-np.arange(16, dtype=np.float32) / np.float32(16))
    t = np.arange(S)
    pos = np.stack([t // GRID_W, t % GRID_W], 1).astype(np.float32)
    ang = (pos[:, :, None] * freqs).reshape(NT, P, 32).transpose(1, 0, 2)
    for n, table in enumerate((np.cos(ang) * MLA_SCALE, np.sin(ang) * MLA_SCALE, np.cos(ang), np.sin(ang))):
        cst[:, C_ROPE + 64 * n:C_ROPE + 64 * n + 64] = table.reshape(P, 64)
    cst[:, C_IOTA:C_IOTA + CAP] = np.arange(CAP)
    rel = np.arange(REL) - (S - 1)
    n = np.abs(rel)
    large = 8 + (np.log(np.maximum(n, 1).astype(np.float32) / np.float32(8)) / np.float32(np.log(128.0)) * 8).astype(np.int32)
    bucket = np.where(rel > 0, 16, 0) + np.where(n < 8, n, np.minimum(large, 15))
    hot = np.zeros((32, 512), np.float32)
    hot[bucket, np.arange(REL)] = 1.0
    many = (n <= 64).astype(int) + (n % 4 == 0) + (n % 16 == 0)
    table = np.zeros((12, 512), np.float32)
    table[DIFF_HEADS:, :REL] = np.where(many > 0, np.log(np.maximum(many, 1)), NEG)
    return {"cst": cst, "bucket_hot": hot, "pattern_log": table}


class Steps:

    def __init__(self, sem, names):
        self.sem, self.names, self.done = sem, list(names), 0

    def __call__(self, name):
        assert self.names[self.done] == name, (self.names[self.done], name)
        self.done += 1
        return 1

    def at(self, name):
        return self.names.index(name) + 1


class Count:

    def __init__(self, sem):
        self.sem, self.n = sem, 0

    def take(self, k):
        self.n += k
        return self.n - k


class Job:

    def __init__(self, mms, evac, on, last_of=()):
        self.mms, self.evac, self.on, self.last_of = mms, evac, on, last_of


def build(nc, A):
    ctx = ExitStack()
    with ctx:
        def sem(name):
            return ctx.enter_context(nc.semaphore(name))

        def sb(name, shape, on=None):
            return (on or ctx).enter_context(nc.sbuf_tensor(name, [P] + list(shape), F32))

        ps = ctx.enter_context(nc.psum_tensor("ps", [P, 8, 512], F32))
        ring = sb("ring", [SLOTS, SLOT])
        cst = sb("cst", [C_ALL])
        vcol = sb("vcol", [160])
        x = sb("x", [NT, D])
        modc = sb("modc", [2, 48, 2])
        small = sb("small", [64])
        zeros = sb("zeros", [P])
        cx = sb("cx", [NT, D])
        kTc = sb("kTc", [KC, S])
        kpeTc = sb("kpeTc", [S])
        vac = sb("vac", [NT, D])
        e_own = sem("moe_own")
        scp = sb("scp", [KC, 32])
        ident = cst[:, C_ID:C_ID + P]
        flip = cst[:, C_FLIP:C_FLIP + P]

        slot_loaded = [sem(f"slot{i}_loaded") for i in range(SLOTS)]
        job_done = Count(sem("job_done"))
        job_act = Count(sem("job_act_evac"))
        job_dve = Count(sem("job_dve_evac"))
        score_done = Count(sem("score_done"))
        max_done = Count(sem("max_done"))
        exp_done = Count(sem("exp_done"))
        probT_done = Count(sem("probT_done"))
        probT_sb = Count(sem("probT_sb"))
        pv_done = Count(sem("pv_done"))
        out_done = Count(sem("out_done"))
        ada_done = Count(sem("ada_done"))
        mlp_used = Count(sem("mlp_piece_used"))
        relu_done = Count(sem("relu_done"))
        square_done = Count(sem("square_done"))

        pieces = []
        released = {}
        loads = [0] * SLOTS
        arrival = {}
        fed = [0]

        def plan(src, cols):
            n = len(pieces)
            pieces.append((src, cols))
            loads[n % SLOTS] += 1
            arrival[n] = 16 * loads[n % SLOTS]
            return n

        class Loop:

            def __init__(self, srcs, turns):
                assert len(srcs) % SLOTS == 0
                self.srcs, self.turns, self.n0, self.used = srcs, turns, len(pieces), {}
                for i in range(len(srcs) * turns):
                    if i < SLOTS:
                        plan(*srcs[i](0))
                    else:
                        loads[len(pieces) % SLOTS] += 1
                        arrival[len(pieces)] = 16 * loads[len(pieces) % SLOTS]
                        pieces.append(None)

            def arrived(self, pe, m, i):
                pe.wait_ge(slot_loaded[(self.n0 + i) % SLOTS], m * (16 * len(self.srcs) // SLOTS) + arrival[self.n0 + i])
                return self.n0 + i

            def uses(self, i, s, value, per_turn):
                self.used[i] = (s, value, per_turn)

            def end(self):
                n = len(self.srcs)
                for i in range(n - SLOTS, n):
                    s, value, per = self.used[i]
                    released[self.n0 + n * (self.turns - 1) + i] = (s, value + (self.turns - 1) * per)

            def feed(self, sp):
                assert fed[0] == self.n0 + SLOTS, (fed[0], self.n0)
                n = len(self.srcs)

                def load(m, i, after, turn):
                    s, value, per = self.used[after]
                    src, cols = self.srcs[i](m)
                    dst = slot(self.n0 + i, cols)
                    if len(src.shape) == 3:
                        dst = dst.rearrange("p (k f) -> p k f", k=src.shape[1])
                    sp.wait_ge(s, turn * per + value)
                    sp.dma_start(dst, src).then_inc(slot_loaded[(self.n0 + i) % SLOTS], 16)
                with sp.Fori(0, self.turns - 1) as m:
                    for i in range(SLOTS, n):
                        load(m, i, i - SLOTS, m)
                    for i in range(SLOTS):
                        load(m + 1, i, n - SLOTS + i, m)
                for i in range(SLOTS, n):
                    load(self.turns - 1, i, i - SLOTS, self.turns - 1)
                fed[0] = self.n0 + n * self.turns

        def slot(n, cols):
            return ring[:, n % SLOTS, 0:cols]

        def feed(sp, limit=None):
            while fed[0] < len(pieces) and (limit is None or fed[0] < limit):
                n = fed[0]
                if pieces[n] is None or (n >= SLOTS and n - SLOTS not in released):
                    return
                if n >= SLOTS:
                    sp.wait_ge(*released[n - SLOTS])
                src, cols = pieces[n]
                dst = slot(n, cols)
                if len(src.shape) == 3:
                    dst = dst.rearrange("p (k f) -> p k f", k=src.shape[1])
                sp.dma_start(dst, src).then_inc(slot_loaded[n % SLOTS], 16)
                fed[0] += 1

        def arrived(pe, n):
            pe.wait_ge(slot_loaded[n % SLOTS], arrival[n])

        class Run:
            def __init__(self, jobs, banks=(0, 1, 2, 3)):
                self.jobs, self.banks = jobs, banks
                self.base = job_done.take(len(jobs))
                self.pos, self.count = [], {"act": 0, "dve": 0}
                self.first = {"act": job_act.take(sum(j.on == "act" for j in jobs)),
                              "dve": job_dve.take(sum(j.on == "dve" for j in jobs))}
                for j in jobs:
                    self.count[j.on] += 1
                    self.pos.append(self.count[j.on])

            def out_of(self, eng, i):
                j = self.jobs[i]
                s = job_act if j.on == "act" else job_dve
                eng.wait_ge(s.sem, self.first[j.on] + self.pos[i])

            def finished(self, eng):
                for on, s in (("act", job_act), ("dve", job_dve)):
                    if self.count[on]:
                        eng.wait_ge(s.sem, self.first[on] + self.count[on])

            def pe(self, pe):
                seen = set()
                for i, j in enumerate(self.jobs):
                    if i >= len(self.banks):
                        self.out_of(pe, i - len(self.banks))
                    bank = ps[:, self.banks[i % len(self.banks)], :]
                    for (rows, lo, hi), lhsT, rhs, start, stop, tr, piece in j.mms:
                        if piece is not None and piece not in seen:
                            arrived(pe, piece)
                            seen.add(piece)
                        if tr:
                            last = nc.tensor.transpose(bank[0:rows, lo:hi], lhsT, rhs)
                        else:
                            last = nc.tensor.matmul(bank[0:rows, lo:hi], lhsT, rhs, start=start, stop=stop)
                    last.then_inc(job_done.sem, 1)
                    for piece in j.last_of:
                        released[piece] = (job_done.sem, self.base + i + 1)

            def ev(self, eng, on):
                for i, j in enumerate(self.jobs):
                    if j.on == on:
                        eng.wait_ge(job_done.sem, self.base + i + 1)
                        s = job_act if on == "act" else job_dve
                        j.evac(ps[:, self.banks[i % len(self.banks)], :]).then_inc(s.sem, 1)

        def to_act(out, scale=1.0, bias=0.0, cols=None):
            return lambda bank: nc.scalar.activation(out, bank if cols is None else bank[:, 0:cols],
                                                     ACT.Identity, bias=bias, scale=scale)

        def to_dve(out, scale=None, bias=None, cols=None):
            def go(bank):
                b = bank if cols is None else bank[:, 0:cols]
                if scale is None and bias is None:
                    return nc.vector.tensor_copy(out, b)
                if bias is None:
                    return nc.vector.tensor_scalar(out, b, scale, None, ALU.mult)
                if scale is None:
                    return nc.vector.tensor_scalar(out, b, bias, None, ALU.add)
                return nc.vector.tensor_scalar(out, b, scale, bias, ALU.mult, ALU.add)
            return go

        def turn(i, out, scale=None, bias=None, cols=None):
            if i % 2 == 0:
                return to_act(out, 1.0 if scale is None else scale, 0.0 if bias is None else bias, cols), "act"
            return to_dve(out, scale, bias, cols), "dve"

        def transposes(n, src, dst, scale=None, bias=None):
            jobs = []
            for c in range(n):
                mms = [((P, t * P, t * P + P), src(t, c), ident, True, True, True, None) for t in range(NT)]
                ev, on = turn(c, dst(c), scale and scale(c), bias and bias(c), S)
                jobs.append(Job(mms, ev, on))
            return jobs

        def vc(i):
            return vcol[:, i:i + 1]

        class Attention:

            def __init__(self, name, units, probs, probsT, fill=None, bank=0):
                self.units, self.probs, self.probsT, self.fill = units, probs, probsT, fill
                self.bank = bank
                n = len(units)
                self.b = {k: c.take(n) for k, c in (("s", score_done), ("m", max_done), ("e", exp_done),
                                                    ("t", probT_done), ("ts", probT_sb), ("pv", pv_done),
                                                    ("o", out_done))}
                self.scaled = 0

            def finished(self, eng):
                eng.wait_ge(out_done.sem, self.b["o"] + len(self.units))

            def pe(self, pe):
                for _ in self.pe_units(pe):
                    pass

            def pe_units(self, pe):
                def scores(u):
                    if u >= 2:
                        pe.wait_ge(exp_done.sem, self.b["e"] + u - 1)
                    for lo, hi, lhsT, rhs, start, stop in self.units[u]["scores"]:
                        last = nc.tensor.matmul(ps[:, self.bank + u % 2, lo:hi], lhsT, rhs, start=start, stop=stop,
                                                skip_group_check=True)
                    last.then_inc(score_done.sem, 1)

                def turn_over(u):
                    nt, nk = self.units[u]["nt"], 4 // self.units[u]["nt"]
                    pe.wait_ge(exp_done.sem, self.b["e"] + u + 1)
                    if u >= 1:
                        pe.wait_ge(probT_sb.sem, self.b["ts"] + u)
                    for t in range(nt):
                        for c in range(nk):
                            col = (c * nt + t) * P
                            last = nc.tensor.transpose(ps[:, self.bank + 2, col:col + P],
                                                       self.probs[:, u % 2, (t * nk + c) * P:(t * nk + c + 1) * P], ident)
                    last.then_inc(probT_done.sem, 1)

                def times_values(u):
                    nt, nk = self.units[u]["nt"], 4 // self.units[u]["nt"]
                    pe.wait_ge(probT_sb.sem, self.b["ts"] + u + 1)
                    if u >= 1:
                        pe.wait_ge(out_done.sem, self.b["o"] + u)
                    for t in range(nt):
                        for c in range(nk):
                            col = (c * nt + t) * P
                            v = self.units[u]["v"](c)
                            o = 256 * (u % 2) + t * P
                            last = nc.tensor.matmul(ps[:, self.bank + 3, o:o + v.shape[1]], self.probsT[:, u % 2, col:col + P],
                                                    v, start=(c == 0), stop=(c == nk - 1))
                    last.then_inc(pv_done.sem, 1)

                scores(0)
                for u in range(len(self.units)):
                    if u + 1 < len(self.units):
                        scores(u + 1)
                    if self.fill is not None:
                        self.fill(pe, u)
                    turn_over(u)
                    if u >= 1:
                        times_values(u - 1)
                    yield u
                times_values(len(self.units) - 1)

            def act(self, act):
                for u, unit in enumerate(self.units):
                    act.wait_ge(max_done.sem, self.b["m"] + u + 1)
                    if u >= 2:
                        act.wait_ge(probT_done.sem, self.b["t"] + u - 1)
                    if u >= 4:
                        act.wait_ge(out_done.sem, self.b["o"] + u - 3)
                    w = 512 // unit["nt"]
                    for t in range(unit["nt"]):
                        last = nc.scalar.activation(self.probs[:, u % 2, t * w:t * w + w], ps[:, self.bank + u % 2, t * w:t * w + w],
                                                    ACT.Exp, bias=small[:, 2 * (u % 4) + t:2 * (u % 4) + t + 1],
                                                    accum_out=small[:, 8 + 2 * (u % 4) + t:9 + 2 * (u % 4) + t])
                    last.then_inc(exp_done.sem, 1)

            def dve(self, dve, own, tally):
                def top(u):
                    nt = self.units[u]["nt"]
                    dve.wait_ge(score_done.sem, self.b["s"] + u + 1)
                    if u >= 4:
                        dve.wait_ge(exp_done.sem, self.b["e"] + u - 3)
                    nc.vector.reduce_max(small[:, 2 * (u % 4):2 * (u % 4) + nt],
                                         ps[:, self.bank + u % 2, :].rearrange("p (t k) -> p t k", t=nt), AX.X,
                                         negate=True).then_inc(max_done.sem, 1)

                def results(u):
                    unit = self.units[u]
                    inv = small[:, 16 + 2 * (u % 2):16 + 2 * (u % 2) + unit["nt"]]
                    dve.wait_ge(pv_done.sem, self.b["pv"] + u + 1)
                    for t in range(unit["nt"]):
                        out = unit["out"](t)
                        o = 256 * (u % 2) + t * P
                        part = ps[:, self.bank + 3, o:o + out.shape[1]]
                        if unit.get("minus") is not None:
                            dve.wait_ge(out_done.sem, self.b["o"] + u)
                            last = nc.vector.scalar_tensor_tensor(out, part, inv[:, t:t + 1], out, ALU.mult, ALU.add)
                        else:
                            last = nc.vector.tensor_scalar(out, part, inv[:, t:t + 1], None, ALU.mult)
                    last.then_inc(out_done.sem, 1)

                top(0)
                for u, unit in enumerate(self.units):
                    if u + 1 < len(self.units):
                        top(u + 1)
                    nt = unit["nt"]
                    dve.wait_ge(probT_done.sem, self.b["t"] + u + 1)
                    if u >= 2:
                        dve.wait_ge(pv_done.sem, self.b["pv"] + u - 1)
                    nc.vector.tensor_copy(self.probsT[:, u % 2, :], ps[:, self.bank + 2, :]).then_inc(probT_sb.sem, 1)
                    inv = small[:, 16 + 2 * (u % 2):16 + 2 * (u % 2) + nt]
                    sums = small[:, 8 + 2 * (u % 4):8 + 2 * (u % 4) + nt]
                    dve.wait_ge(exp_done.sem, self.b["e"] + u + 1)
                    if u >= 2:
                        dve.wait_ge(out_done.sem, self.b["o"] + u - 1)
                    nc.vector.reciprocal(inv, sums).then_inc(own, 1)
                    tally[0] += 1
                    dve.wait_ge(own, tally[0])
                    if unit.get("minus") is not None:
                        nc.vector.tensor_scalar(inv, inv, unit["minus"], None, ALU.mult).then_inc(own, 1)
                        tally[0] += 1
                        dve.wait_ge(own, tally[0])
                    if u >= 1:
                        results(u - 1)
                results(len(self.units) - 1)

        dve_own = sem("dve_own")
        dve_count = [0]

        def link(dve, ins):
            dve_count[0] += 1
            ins.then_inc(dve_own, 1)
            dve.wait_ge(dve_own, dve_count[0])

        def view(tile, a, b):
            return tile[:, :, :].rearrange("p k s -> p (k s)")[:, 0:a * b].rearrange("p (a b) -> p a b", a=a)

        def rms_names(n):
            return [f"sq{i}" for i in range(n)] + ["sd"]

        def rms_act(act, acts, dves, srcs, junk, at):
            for i, src in enumerate(srcs):
                nc.scalar.activation(junk[:, 0:src.shape[1]], src, ACT.Square,
                                     accum_out=small[:, at + i:at + i + 1]).then_inc(acts.sem, acts(f"sq{i}"))
                act.wait_ge(acts.sem, acts.at(f"sq{i}"))
            act.wait_ge(dves.sem, dves.at("var"))
            nc.scalar.activation(small[:, at:at + len(srcs)], small[:, at:at + len(srcs)], ACT.Sqrt)\
              .then_inc(acts.sem, acts("sd"))

        def rms_dve(dve, acts, dves, groups, at):
            n = sum(g[0] for g in groups)
            dve.wait_ge(acts.sem, acts.at(f"sq{n - 1}"))
            i = at
            for count, width, eps in groups:
                last = nc.vector.tensor_scalar(small[:, i:i + count], small[:, i:i + count], 1.0 / width, eps,
                                               ALU.mult, ALU.add)
                i += count
            last.then_inc(dves.sem, dves("var"))
            dve.wait_ge(acts.sem, acts.at("sd"))
            link(dve, nc.vector.reciprocal(small[:, at:at + n], small[:, at:at + n]))

        def ln_dve(dve, acts, dves, y, gain, shift, stats, which=""):
            for t in range(NT):
                for h in range(2):
                    link(dve, nc.vector.bn_stats(stats[:, t, 6 * h:6 * h + 6], y[:, t, 512 * h:512 * h + 512]))
                link(dve, nc.vector.bn_aggr(stats[:, t, 12:14], stats[:, t, 0:12]))
            var = stats[:, :, 13:14]
            nc.vector.tensor_scalar(small[:, 40:42], var.rearrange("p t o -> p (t o)"), 1e-5, None, ALU.add)\
              .then_inc(dves.sem, dves("ln_var" + which))
            dve.wait_ge(acts.sem, acts.at("ln_sd" + which))
            link(dve, nc.vector.reciprocal(small[:, 42:44], small[:, 42:44]))
            for t in range(NT):
                link(dve, nc.vector.tensor_scalar(y[:, t, :], y[:, t, :], stats[:, t, 12:13], small[:, 42 + t:43 + t],
                                                  ALU.subtract, ALU.mult))
                link(dve, nc.vector.tensor_tensor(y[:, t, :], y[:, t, :], gain, ALU.mult))
                link(dve, nc.vector.tensor_tensor(y[:, t, :], y[:, t, :], shift, ALU.add))

        def ln_act(act, acts, dves, which=""):
            act.wait_ge(dves.sem, dves.at("ln_var" + which))
            nc.scalar.activation(small[:, 42:44], small[:, 40:42], ACT.Sqrt).then_inc(acts.sem, acts("ln_sd" + which))

        ada_w = A["ada_w_2"]
        ada_ids = [[], []]

        def plan_ada(layer):
            for half in range(2):
                for k in range(KC):
                    ada_ids[layer].append(plan(ada_w[layer, k * P:(k + 1) * P, half * N_IN:(half + 1) * N_IN], N_IN))

        def ada_piece(pe, layer, i, base):
            n = ada_ids[layer][i]
            half, k = divmod(i, KC)
            arrived(pe, n)
            for b in range(6):
                j = b % 4
                last = nc.tensor.matmul(ps[32 * j:32 * j + 32, 4 + 2 * half + b // 4, :], scp[:, k, :],
                                        slot(n, N_IN)[:, 512 * b:512 * b + 512], start=(k == 0), stop=(k == KC - 1))
            last.then_inc(ada_done.sem, 1)
            released[n] = (ada_done.sem, base + i + 1)

        def ada_jobs(layer, rows):
            runs = []
            for half in range(2):
                for b, parts in ((0, 128), (1, 64)):
                    q = 2 * half + b
                    chunk = 24 * half + 16 * b
                    mms = [((P, P * c, P * c + parts), rows[0:parts, q, P * c:P * c + P], ident[0:parts, 0:parts],
                            True, True, True, None) for c in range(4)]

                    def ev(bank, chunk=chunk, nj=parts // 32):
                        src = bank.rearrange("p (c j s) -> p j c s", c=4, j=4)[:, 0:nj, :, 0:2]
                        dst = modc[:, layer, chunk:chunk + 4 * nj, :].rearrange("p (j c) s -> p j c s", c=4)
                        add = vcol[:, V_ADA + 48 * layer + chunk:V_ADA + 48 * layer + chunk + 4 * nj]\
                            .rearrange("p (j c o) -> p j c o", c=4, o=1).to_broadcast([P, nj, 4, 2])
                        return nc.vector.tensor_tensor(dst, src, add, ALU.add)
                    runs.append(Job(mms, ev, "dve"))
            return runs

        def mod(layer, which, c, stream):
            return modc[:, layer, which * KC + c, stream:stream + 1]

        w_in = A["w_in"]
        id_in = [plan(w_in[0, k * P:(k + 1) * P, :], N_IN) for k in range(KC)]
        plan_ada(0)
        w_out = A["w_out"].rearrange("l (k p) f -> l p k f", p=P)

        def plan_square(w):
            where = {}
            for lo, hi in ((0, 3), (3, 6), (6, 8)):
                n = plan(w[:, lo:hi, :], (hi - lo) * D)
                for k in range(lo, hi):
                    where[k] = (n, k - lo)
            return where

        id_out = plan_square(w_out[0])

        def sq_at(where, k, lo, hi):
            n, r = where[k]
            return slot(n, SLOT)[:, r * D + lo:r * D + hi]

        small_loaded = sem("small_loaded")
        x_loaded = sem("x_loaded")
        cx_loaded = sem("ctx_loaded")
        wr_loaded = sem("w_router_loaded")
        w_r = sb("w_r", [KC, N_EXPERTS])
        table_dram = nc.dram_tensor("bias_table", [12, 512], F32).ap()

        first = ExitStack()
        h = sb("h", [NT, D], first)
        hT = sb("hT", [KC, S], first)
        early = ExitStack()
        qkT = sb("qkT", [16, S], early)
        vv = sb("vv", [NT, D], early)
        window = sb("window", [12, WIN], early)
        probs = sb("probs", [2, 512], early)
        probsT = sb("probsT", [2, 512], early)
        vrow = sb("vrow", [2, P], early)
        hot = sb("hot", [512], early)
        rel_b = sb("rel_b", [12], early)
        plog = sb("plog", [512], early)
        lamv = sb("lamv", [4, HD], early)
        junk = view(probs, 1, D)[:, 0, :]
        a1 = Steps(sem("p1_act"), ["silu"] + rms_names(NT) + ["lam"])
        v1 = Steps(sem("p1_dve"), ["cols", "var", "h0", "h1", "lamsum", "scp"])
        t1 = sem("p1_table_stored")
        win_loaded = sem("window_loaded")

        vjobs = [Job([((P, 0, P), vrow[:, 0, :], ident, True, True, True, None)], to_dve(vcol[:, 0:P], cols=P), "dve"),
                 Job([((P, 0, V_ALL - P), vrow[0:V_ALL - P, 1, :], ident[0:V_ALL - P, 0:V_ALL - P], True, True, True, None)],
                     to_dve(vcol[:, P:V_ALL], cols=V_ALL - P), "dve"),
                 Job([((12, 0, REL), rel_b[0:32, :], hot[0:32, 0:REL], True, True, False, None)],
                     lambda bank: nc.vector.tensor_tensor(plog[0:12, 0:REL], bank[0:12, 0:REL], plog[0:12, 0:REL], ALU.add),
                     "dve")]
        run_v = Run(vjobs)
        run_h = Run(transposes(KC, lambda t, c: h[:, t, c * P:(c + 1) * P], lambda c: hT[:, c, :],
                               scale=lambda c: vc(V_N1 + c)))

        def projections():
            jobs = []
            cols = [0, 512, 1536, 2048]
            for n in range(16):
                lo = cols[n // 4] + (n % 4) * P
                mms = [((P, 0, S), slot(id_in[k], N_IN)[:, lo:lo + P], hT[:, k, :], k == 0, k == KC - 1, False, id_in[k])
                       for k in range(KC)]
                ev, on = turn(n, qkT[:, n, :], HD ** -0.5 if n // 4 in (0, 2) else None, None, S)
                jobs.append(Job(mms, ev, on))
            for n, lo in enumerate((1024, 2560)):
                for t in range(NT):
                    mms = [((P, 0, 512), hT[:, k, t * P:(t + 1) * P], slot(id_in[k], N_IN)[:, lo:lo + 512],
                            k == 0, k == KC - 1, False, id_in[k]) for k in range(KC)]
                    ev, on = turn(t, vv[:, t, 512 * n:512 * n + 512])
                    jobs.append(Job(mms, ev, on, id_in if (n, t) == (1, 1) else ()))
            return jobs

        run_p = Run(projections(), (0, 1, 2, 3, 4, 5, 6, 7))

        x_dram = A["x"].rearrange("b (t p) d -> p (b t) d", p=P)
        with nc.Block(no_gpsimd_drain=True) as block:
            @block.tensor
            def _(pe):
                pe.wait_ge(small_loaded, 16 * 17)
                run_v.pe(pe)
                run_v.finished(pe)
                pe.wait_ge(v1.sem, v1.at("h1"))
                run_h.pe(pe)
                run_h.finished(pe)
                run_p.pe(pe)

            @block.sync
            def _(sp):
                sp.dma_start(x[:, :, :], x_dram).then_inc(x_loaded, 16)
                feed(sp, 2)
                sp.wait_ge(small_loaded, 16 * 17)
                feed(sp, SLOTS)
                sp.dma_start(cx[:, :, :], A["ctx_2"].rearrange("b (t p) d -> p (b t) d", p=P)).then_inc(cx_loaded, 16)
                run_v.finished(sp)
                sp.dma_start(table_dram, plog[0:12, :]).then_inc(t1, 16)
                sp.wait_ge(t1, 16)
                src = bass.AP(tensor=table_dram.tensor, offset=table_dram.offset, ap=[[1, P], [512, 12], [1, WIN]])
                sp.dma_start(window[:, :, :], src).then_inc(win_loaded, 16)
                feed(sp)

            @block.scalar
            def _(act):
                def load(dst, src):
                    act.dma_start(dst, src).then_inc(small_loaded, 16)
                load(cst[:, :], A["cst"])
                rows = [("ada_b_2", V_ADA, 96), ("norm1_g", V_N1, 8), ("norm2_g", V_N2, 8), ("c_2", V_C, 8),
                        ("c_ctx_2", V_C + 8, 8), ("subln_g", V_SUB, 1), ("mla_q_norm_2", V_QN, 4),
                        ("mla_kv_norm_2", V_KVN, 2), ("na_b_qkv_2", V_BQKV, 24)]
                for name, at, n in rows:
                    a = A[name]
                    a = a.rearrange("(n f) -> n f", f=P) if len(a.shape) == 1 else a.rearrange("l (n f) -> (l n) f", f=P)
                    load(vrow[at % P:at % P + n, at // P, :], a)
                load(hot[0:32, :], A["bucket_hot"])
                act.dma_start(w_r[:, :, :], A["w_router"].rearrange("l (k p) e -> p (l k) e", p=P)).then_inc(wr_loaded, 16)
                load(plog[0:12, :], A["pattern_log"])
                load(rel_b[0:32, :], A["rel_bias"])
                for i, name in enumerate(("lam_q1", "lam_k1", "lam_q2", "lam_k2")):
                    load(lamv[:, i, :], A[name].partition_broadcast(P))
                act.wait_ge(x_loaded, 16)
                act.wait_ge(v1.sem, v1.at("cols"))
                nc.scalar.activation(small[:, 44:60], vcol[:, V_C:V_C + 16], ACT.Exp, scale=-1.0)\
                  .then_inc(a1.sem, a1("silu"))
                rms_act(act, a1, v1, [x[:, t, :] for t in range(NT)], junk, 0)
                act.wait_ge(v1.sem, v1.at("lamsum"))
                nc.scalar.activation(small[:, 4:6], small[:, 4:6], ACT.Exp).then_inc(a1.sem, a1("lam"))
                run_h.ev(act, "act")
                run_p.ev(act, "act")

            @block.vector
            def _(dve):
                run_v.ev(dve, "dve")
                run_v.finished(dve)
                nc.vector.memset(zeros[:, :], 0.0)
                nc.vector.memset(scp[:, :, :], 0.0).then_inc(v1.sem, v1("cols"))
                dve.wait_ge(x_loaded, 16)
                rms_dve(dve, a1, v1, [(NT, D, 1e-6)], 0)
                for t in range(NT):
                    nc.vector.tensor_scalar(h[:, t, :], x[:, t, :], small[:, t:t + 1], None, ALU.mult)\
                      .then_inc(v1.sem, v1(f"h{t}"))
                lam4 = lamv[:, :, :].rearrange("p (a b) d -> p a b d", a=2)
                link(dve, nc.vector.tensor_tensor(lam4[:, :, 0, :], lam4[:, :, 0, :], lam4[:, :, 1, :], ALU.mult))
                nc.vector.reduce_sum(small[:, 4:6], lam4[:, :, 0, :], AX.X).then_inc(v1.sem, v1("lamsum"))
                dve.wait_ge(a1.sem, a1.at("silu"))
                link(dve, nc.vector.tensor_scalar(small[:, 44:60], small[:, 44:60], 1.0, None, ALU.add))
                link(dve, nc.vector.reciprocal(small[:, 44:60], small[:, 44:60]))
                dve.wait_ge(v1.sem, v1.at("cols"))
                nc.vector.tensor_tensor(scp[:, :, 0:2], vcol[:, V_C:V_C + 16].rearrange("p (s k) -> p k s", s=2),
                                        small[:, 44:60].rearrange("p (s k) -> p k s", s=2), ALU.mult)\
                  .then_inc(v1.sem, v1("scp"))
                dve.wait_ge(a1.sem, a1.at("lam"))
                link(dve, nc.vector.tensor_tensor(small[:, 24:25], small[:, 5:6], small[:, 4:5], ALU.subtract))
                link(dve, nc.vector.tensor_scalar(small[:, 25:26], small[:, 24:25], -0.2, None, ALU.add))
                run_h.ev(dve, "dve")
                run_p.ev(dve, "dve")

        def unit1(q, k, hh, table, v, out, minus=None):
            lo = HD * (hh % 2)
            sc = []
            for t in range(NT):
                sc.append((t * S, t * S + S, qkT[lo:lo + HD, q, t * P:(t + 1) * P], qkT[lo:lo + HD, k, :], True, False))
                off = P * (1 - t)
                sc.append((t * S, t * S + S, flip, window[:, table, off:off + S], False, True))
            return {"nt": NT, "scores": sc, "v": v, "out": out, "minus": minus}

        mix = h
        units = []
        for hh in range(DIFF_HEADS):
            for s in range(2):
                units.append(unit1(hh, 4 + hh, s, hh, lambda c, hh=hh: vv[:, c, P * hh:P * hh + P],
                                   lambda t, hh=hh: mix[:, t, P * hh:P * hh + P],
                                   small[:, 25:26] if s else None))
        for hh in range(DIL_HEADS):
            units.append(unit1(8 + hh // 2, 12 + hh // 2, hh, DIFF_HEADS + hh,
                               lambda c, hh=hh: vv[:, c, 512 + HD * hh:512 + HD * hh + HD],
                               lambda t, hh=hh: mix[:, t, 512 + HD * hh:512 + HD * hh + HD]))
        ada_base = ada_done.take(16)
        att1 = Attention("a1", units, probs, probsT, fill=lambda pe, u: ada_piece(pe, 0, u, ada_base))
        with nc.Block(no_gpsimd_drain=True) as block:
            @block.tensor
            def _(pe):
                pe.wait_ge(win_loaded, 16)
                att1.pe(pe)

            @block.sync
            def _(sp):
                feed(sp)

            @block.scalar
            def _(act):
                att1.act(act)

            @block.vector
            def _(dve):
                att1.dve(dve, dve_own, dve_count)
        early.close()

        gate_d = A["w_gate"].rearrange("l e k f -> (l e k) f")
        up_d = A["w_up"].rearrange("l e k f -> (l e k) f")
        down_d = A["w_down"].rearrange("l e k f -> (l e k) f")
        PIECES = 24

        def moe_piece(e, i):
            if i < 2 * KC:
                src = (gate_d, up_d)[i % 2]
                return src[bass.ds(e * D + (i // 2) * P, P), :], D_FF
            c = 3 * (i - 2 * KC)
            n = min(3, FCH - c)
            return down_d[bass.ds(e * D_FF + c * P, n * P), :].rearrange("(c p) f -> p c f", p=P), n * D

        def mla_sources():
            dq = A["mla_w_dq_2"].rearrange("l (k p) f -> p (l k) f", p=P)
            uq = A["mla_w_uq_2"].rearrange("l (k p) f -> p (l k) f", p=P)
            return {"dq": [(dq[:, 4 * i:4 * i + 4, :], 4 * Q_RANK) for i in range(2)],
                    "dkv": [(A["mla_w_dkv_2"].rearrange("l (k p) f -> p (l k) f", p=P), KC * (KV_RANK + ROPE))],
                    "uq": [(uq[:, 2 * i:2 * i + 2, :], 2 * MLA_HEADS * (NOPE + ROPE)) for i in range(2)],
                    "ukv": [(A["mla_w_ukv_2"][0, k * P:(k + 1) * P, :], 2 * D) for k in range(2)]}

        def plan_mla(ids, *names):
            for name in names:
                if name == "o":
                    ids["o"] = plan_square(A["mla_w_o_2"].rearrange("l (k p) f -> p (l k) f", p=P))
                else:
                    ids[name] = [plan(*src) for src in mla_sources()[name]]

        GROUPS = D_FF2 // (2 * P)

        def mlp_piece(layer, w, g):
            if w == 1:
                return A["mlp_w1_2"][layer].rearrange("(k p) f -> p k f", p=P)[:, :, bass.ds(g * (2 * P), 2 * P)], KC * 2 * P
            return A["mlp_w2_2"][layer, bass.ds(g * (2 * P), 2 * P), :].rearrange("(k p) f -> p k f", p=P), 2 * D

        LEAD, PAIRS = 5, GROUPS // 4
        CTX_AFTER = {(0, 4): ("dq", "dkv"), (1, 2): ("uq",), (1, 8): ("ukv",), (3, 6): ("o",)}
        MLP_AFTER = {2: (1, 0), 6: (2, 0), 9: (1, 1), 13: (2, 1)}
        ids_c, moe_ids = {}, {}

        def plan_expert(e):
            for i in range(PIECES):
                moe_ids[e, i] = plan(*moe_piece(e, i))
                plan_mla(ids_c, *CTX_AFTER.get((e, i), ()))

        for e in range(LEAD):
            plan_expert(e)
        pair_srcs, pair_at = [], {}
        for d in range(2):
            for i in range(PIECES):
                pair_at[d, i] = len(pair_srcs)
                pair_srcs.append(lambda m, d=d, i=i: moe_piece(m * 2 + (LEAD + d), i))
                if i in MLP_AFTER:
                    w, g = MLP_AFTER[i]
                    pair_at[d, "mlp", i] = len(pair_srcs)
                    pair_srcs.append(lambda m, w=w, g=2 * d + g: mlp_piece(0, w, m * 4 + g))
        pairs = Loop(pair_srcs, PAIRS)
        AFTER_PAIRS = LEAD + 2 * PAIRS
        plan_expert(AFTER_PAIRS)
        FINAL = AFTER_PAIRS + 1
        finals = Loop([lambda m, i=i: moe_piece(m + FINAL, i) for i in range(PIECES)], N_EXPERTS - FINAL)
        ids_x = {}
        plan_mla(ids_x, "dq", "dkv", "uq", "ukv")
        plan_ada(1)
        plan_mla(ids_x, "o")
        TURN = 4
        ORDER = [(1, 0), (1, 1), (2, 0), (1, 2), (2, 1), (1, 3), (2, 2), (2, 3)]

        def plan_mlp(layer):
            return Loop([lambda m, w=w, g=g: mlp_piece(layer, w, m * TURN + g) for w, g in ORDER], GROUPS // TURN)

        mlp_x = plan_mlp(0)
        w_qkv = A["na_w_qkv_2"]
        id_na = [plan(w_qkv[0, k * P:(k + 1) * P, :], N_IN) for k in range(KC)]
        id_nao = plan_square(A["na_w_o_2"].rearrange("l (k p) f -> p (l k) f", p=P))
        mlp_n = plan_mlp(1)

        keep = ExitStack()
        xeT = sb("xeT", [KC, N_EXPERTS * CAP], keep)
        gT = sb("gT", [N_EXPERTS, S], keep)
        mid = ExitStack()
        rows0 = view(vac, 4, 512)
        sq = view(kTc, 4, 512)[:, 0:2, :]
        sel = sb("sel", [NT, N_EXPERTS, CAP], mid)
        selg = sb("selg", [NT, N_EXPERTS, 4, CAP], mid)
        lg = sb("lg", [NT, 16], mid)
        aff = sb("aff", [NT, 16], mid)
        affT = sb("affT", [S], mid)
        work = sb("work", [S], mid)
        maskT = sb("maskT", [S], mid)
        top8 = sb("top8", [8], mid)
        slotT = sb("slotT", [NT, 16], mid)
        junk = view(kTc, 2, D)[:, 1, :]
        scol = sb("scol", [8], mid)
        a2 = Steps(sem("p2_act"), ["row0", "row2", "subsd"] + rms_names(NT) + ["ra"])
        v2 = Steps(sem("p2_dve"), ["row1", "row3", "subvar", "sub", "var", "h", "lmax", "aff", "slot", "sel"])

        def row_out(q, rows, parts, eng):
            out, src = rows[0:parts, q, :], ps[0:parts, 4 + q, :]
            return nc.scalar.activation(out, src, ACT.Identity) if eng == "act" else nc.vector.tensor_copy(out, src)

        run_ada = Run(ada_jobs(0, rows0))
        run_m = Run(transposes(KC, lambda t, c: mix[:, t, c * P:(c + 1) * P], lambda c: hT[:, c, :],
                               scale=lambda c: scol[:, c:c + 1]))

        def out_jobs():
            jobs = []
            for t in range(NT):
                for half in range(2):
                    mms = [((P, 0, 512), hT[:, k, t * P:(t + 1) * P], sq_at(id_out, k, 512 * half, 512 * half + 512),
                            k == 0, k == KC - 1, False, id_out[k][0]) for k in range(KC)]
                    part = x[:, t, 512 * half:512 * half + 512]
                    jobs.append(Job(mms, lambda bank, part=part: nc.vector.tensor_tensor(part, bank, part, ALU.add),
                                    "dve", [id_out[k][0] for k in (0, 3, 6)] if (t, half) == (1, 1) else ()))
            return jobs

        run_o = Run(out_jobs(), (4, 5, 6, 7))
        run_h2 = Run(transposes(KC, lambda t, c: h[:, t, c * P:(c + 1) * P], lambda c: hT[:, c, :],
                                scale=lambda c: vc(V_N2 + c)))
        run_r = Run([Job([((P, t * 16, t * 16 + 16), hT[:, k, t * P:(t + 1) * P], w_r[:, k, :], k == 0, k == KC - 1,
                           False, None) for t in range(NT) for k in range(KC)],
                         lambda bank: nc.vector.tensor_copy(lg[:, :, :].rearrange("p t e -> p (t e)"), bank[:, 0:32]), "dve")])
        run_at = Run([Job([((16, t * P, t * P + P), aff[:, t, :], ident, True, True, True, None) for t in range(NT)],
                          lambda bank: nc.vector.tensor_copy(affT[0:16, :], bank[0:16, 0:S]), "dve")])
        run_st = Run([Job([((P, t * 16, t * 16 + 16), work[0:16, t * P:(t + 1) * P], ident[0:16, 0:16], True, True, True, None)
                           for t in range(NT)],
                          lambda bank: nc.vector.tensor_copy(slotT[:, :, :].rearrange("p t e -> p (t e)"), bank[:, 0:32]),
                          "dve")])

        def gather_jobs():
            jobs = []
            for c in range(KC):
                mms = [((P, 0, 512), h[:, t, c * P:(c + 1) * P], sel[:, t, :, :].rearrange("p e s -> p (e s)"),
                        t == 0, t == NT - 1, False, None) for t in range(NT)]
                ev, on = turn(c, xeT[:, c, :], vc(V_N2 + c))
                jobs.append(Job(mms, ev, on))
            for e in range(0, N_EXPERTS, 2):
                mms = [((P, 256 * d + t * P, 256 * d + t * P + P), selg[:, t, e + d, :, :].rearrange("p j s -> p (j s)"),
                        ident, True, True, True, None) for d in range(2) for t in range(NT)]
                ev, on = turn(e // 2, gT[:, e:e + 2, :].rearrange("p e s -> p (e s)"))
                jobs.append(Job(mms, ev, on))
            return jobs

        run_g = Run(gather_jobs(), (0, 1, 2, 3, 4, 5, 6, 7))

        with nc.Block(no_gpsimd_drain=True) as block:
            @block.tensor
            def _(pe):
                pe.wait_ge(a2.sem, a2.at("row2"))
                pe.wait_ge(v2.sem, v2.at("row3"))
                run_ada.pe(pe)
                run_ada.finished(pe)
                pe.wait_ge(v2.sem, v2.at("sub"))
                run_m.pe(pe)
                run_m.finished(pe)
                run_o.pe(pe)
                pe.wait_ge(v2.sem, v2.at("h"))
                run_h2.pe(pe)
                run_h2.finished(pe)
                pe.wait_ge(wr_loaded, 16)
                run_r.pe(pe)
                pe.wait_ge(v2.sem, v2.at("aff"))
                run_at.pe(pe)
                pe.wait_ge(v2.sem, v2.at("slot"))
                run_st.pe(pe)
                pe.wait_ge(v2.sem, v2.at("sel"))
                run_g.pe(pe)

            @block.sync
            def _(sp):
                feed(sp)

            @block.scalar
            def _(act):
                row_out(0, rows0, 128, "act").then_inc(a2.sem, a2("row0"))
                row_out(2, rows0, 128, "act").then_inc(a2.sem, a2("row2"))
                act.wait_ge(v2.sem, v2.at("subvar"))
                nc.scalar.activation(small[:, 32:40], small[:, 24:32], ACT.Sqrt).then_inc(a2.sem, a2("subsd"))
                run_m.ev(act, "act")
                run_o.finished(act)
                rms_act(act, a2, v2, [x[:, t, :] for t in range(NT)], junk, 0)
                run_h2.ev(act, "act")
                act.wait_ge(v2.sem, v2.at("lmax"))
                for t in range(NT):
                    last = nc.scalar.activation(aff[:, t, :], lg[:, t, :], ACT.Exp, bias=small[:, 50 + t:51 + t],
                                                accum_out=small[:, 52 + t:53 + t])
                last.then_inc(a2.sem, a2("ra"))
                run_g.ev(act, "act")

            @block.vector
            def _(dve):
                row_out(1, rows0, 64, "dve").then_inc(v2.sem, v2("row1"))
                row_out(3, rows0, 64, "dve").then_inc(v2.sem, v2("row3"))
                link(dve, nc.vector.tensor_tensor(sq[:, :, :], mix[:, :, 0:512], mix[:, :, 0:512], ALU.mult))
                link(dve, nc.vector.reduce_sum(small[:, 24:32], sq[:, :, :].rearrange("p t (h f) -> p (t h) f", f=P), AX.X))
                nc.vector.tensor_scalar(small[:, 24:32], small[:, 24:32], 1.0 / P, 1e-5, ALU.mult, ALU.add)\
                  .then_inc(v2.sem, v2("subvar"))
                nc.vector.memset(scol[:, 4:8], 1.0)
                nc.vector.tensor_scalar(scol[:, 0:4], vc(V_SUB).to_broadcast([P, 4]), 1.0 - 0.2, None, ALU.mult)
                dve.wait_ge(a2.sem, a2.at("subsd"))
                link(dve, nc.vector.reciprocal(small[:, 32:40], small[:, 32:40]))
                for t in range(NT):
                    heads = mix[:, t, 0:512].rearrange("p (h f) -> p h f", f=P)
                    inv = small[:, 32 + 4 * t:36 + 4 * t].rearrange("p (h o) -> p h o", o=1).to_broadcast([P, 4, P])
                    last = nc.vector.tensor_tensor(heads, heads, inv, ALU.mult)
                last.then_inc(v2.sem, v2("sub"))
                run_ada.ev(dve, "dve")
                run_ada.finished(dve)
                for i in (1, 4):
                    part = modc[:, 0, 8 * i:8 * i + 8, :]
                    link(dve, nc.vector.tensor_scalar(part, part, 1.0, None, ALU.add))
                run_m.ev(dve, "dve")
                run_o.ev(dve, "dve")
                run_o.finished(dve)
                rms_dve(dve, a2, v2, [(NT, D, 1e-6)], 0)
                for t in range(NT):
                    last = nc.vector.tensor_scalar(h[:, t, :], x[:, t, :], small[:, t:t + 1], None, ALU.mult)
                last.then_inc(v2.sem, v2("h"))
                run_h2.ev(dve, "dve")
                run_r.ev(dve, "dve")
                run_r.finished(dve)
                nc.vector.reduce_max(small[:, 50:52], lg[:, :, :], AX.X, negate=True).then_inc(v2.sem, v2("lmax"))
                dve.wait_ge(a2.sem, a2.at("ra"))
                link(dve, nc.vector.reciprocal(small[:, 52:54], small[:, 52:54]))
                for t in range(NT):
                    last = nc.vector.tensor_scalar(aff[:, t, :], aff[:, t, :], small[:, 52 + t:53 + t], None, ALU.mult)
                last.then_inc(v2.sem, v2("aff"))
                run_at.ev(dve, "dve")
                run_at.finished(dve)
                src = affT
                for r in range(CAP // 8):
                    dst = work if r % 2 == 0 else maskT
                    link(dve, nc.vector.max(top8[0:16, :], src[0:16, :]))
                    link(dve, nc.vector.match_replace(dst[0:16, :], top8[0:16, :], src[0:16, :], -1.0))
                    src = dst
                link(dve, nc.vector.tensor_scalar(work[0:16, :], maskT[0:16, :], 0.0, None, ALU.is_lt))
                link(dve, nc.vector.tensor_tensor_scan(affT[0:16, :], work[0:16, :], work[0:16, :], 0.0, ALU.add, ALU.max))
                link(dve, nc.vector.tensor_tensor(affT[0:16, :], affT[0:16, :], work[0:16, :], ALU.mult))
                nc.vector.tensor_scalar(work[0:16, :], affT[0:16, :], -1.0, None, ALU.add).then_inc(v2.sem, v2("slot"))
                run_st.ev(dve, "dve")
                run_st.finished(dve)
                iota = cst[:, C_IOTA:C_IOTA + CAP].rearrange("p (o s) -> p o s", o=1).to_broadcast([P, N_EXPERTS, CAP])
                for t in range(NT):
                    slots = slotT[:, t, :].rearrange("p (e o) -> p e o", o=1).to_broadcast([P, N_EXPERTS, CAP])
                    last = nc.vector.tensor_tensor(sel[:, t, :, :], slots, iota, ALU.is_equal)
                link(dve, last)
                for t in range(NT):
                    s4 = sel[:, t, :, :].rearrange("p e (o s) -> p e o s", o=1).to_broadcast([P, N_EXPERTS, 4, CAP])
                    a4 = aff[:, t, :].rearrange("p (e o q) -> p e o q", o=1, q=1).to_broadcast([P, N_EXPERTS, 4, CAP])
                    last = nc.vector.tensor_tensor(selg[:, t, :, :, :], s4, a4, ALU.mult)
                last.then_inc(v2.sem, v2("sel"))
                run_g.ev(dve, "dve")
        mid.close()

        ln_loaded = Count(sem("ln_loaded"))
        streams = (x, cx)

        def modulated(layer, which, s, dst, off=0):
            y = streams[s]
            return transposes(KC, lambda t, c: y[:, t, c * P:(c + 1) * P], lambda c: dst[:, c, off:off + S],
                              scale=lambda c: mod(layer, which + 1, c, s), bias=lambda c: mod(layer, which, c, s))

        def gate_jobs(layer, which, s, gB):
            jobs = []
            for half in range(2):
                mms = [((P, c * P, c * P + P), mod(layer, which, 4 * half + c, s).to_broadcast([P, P]), ident,
                        True, True, False, None) for c in range(4)]
                ev, on = turn(half, gB[:, 512 * half:512 * half + 512])
                jobs.append(Job(mms, ev, on))
            return jobs

        def load_ln(act, which, layer, lnb):
            for i, g in enumerate("gb"):
                act.dma_start(lnb[:, i, :], A[f"ln{which}_{g}_2"][layer:layer + 1, :].partition_broadcast(P)
                              .rearrange("q o d -> q (o d)")).then_inc(ln_loaded.sem, 16)
            ln_loaded.take(32)

        def gated(bank, part, gate):
            link(nc.vector, nc.vector.tensor_tensor(bank, bank, gate, ALU.mult))
            return nc.vector.scalar_tensor_tensor(part, part, ALPHA, bank, ALU.mult, ALU.add)

        def square_jobs(oT, where, s, gB):
            jobs = []
            for t in range(NT):
                for half in range(2):
                    mms = [((P, 0, 512), oT[:, k, t * P:(t + 1) * P], sq_at(where, k, 512 * half, 512 * half + 512),
                            k == 0, k == KC - 1, False, where[k][0]) for k in range(KC)]
                    part = streams[s][:, t, 512 * half:512 * half + 512]
                    gate = gB[:, 512 * half:512 * half + 512]
                    jobs.append(Job(mms, lambda bank, part=part, gate=gate: gated(bank, part, gate), "dve",
                                    [where[k][0] for k in (0, 3, 6)] if (t, half) == (1, 1) else ()))
            return jobs

        class LatentAttention:

            def __init__(self, s, ids, buf, banks):
                self.s, self.buf = s, buf
                name = f"mla{s}"
                hT, qT, cq, ckv, kpe, cqT, ckvT, qpe, qpeT = (buf[k] for k in
                                                              ("hT", "qT", "cq", "ckv", "kpe", "cqT", "ckvT", "qpe", "qpeT"))
                kT, kpeT, va = (kTc, kpeTc, vac) if s else (buf["kT"], buf["kpeT"], buf["va"])
                self.run_t = Run(modulated(0, 0, s, hT), banks)
                jobs = []
                for t in range(NT):
                    mms = [((P, 0, Q_RANK), hT[:, k, t * P:(t + 1) * P],
                            slot(ids["dq"][k // 4], 4 * Q_RANK)[:, (k % 4) * Q_RANK:(k % 4 + 1) * Q_RANK],
                            k == 0, k == KC - 1, False, ids["dq"][k // 4]) for k in range(KC)]
                    ev, on = turn(t, cq[:, t, :])
                    jobs.append(Job(mms, ev, on, ids["dq"] if t else ()))
                w = KV_RANK + ROPE
                for t in range(NT):
                    mms = [((P, 0, w), hT[:, k, t * P:(t + 1) * P], slot(ids["dkv"][0], KC * w)[:, k * w:(k + 1) * w],
                            k == 0, k == KC - 1, False, ids["dkv"][0]) for k in range(KC)]
                    ev, on = turn(t, ckv[:, t, :], cols=w)
                    jobs.append(Job(mms, ev, on, ids["dkv"] if t else ()))
                self.run_d = Run(jobs, banks)
                self.run_c = Run(transposes(4, lambda t, c: cq[:, t, c * P:(c + 1) * P], lambda c: cqT[:, c, :],
                                            scale=lambda c: vc(V_QN + c))
                                 + transposes(2, lambda t, c: ckv[:, t, c * P:(c + 1) * P], lambda c: ckvT[:, c, :],
                                              scale=lambda c: vc(V_KVN + c))
                                 + transposes(1, lambda t, c: kpe[:, t, :], lambda c: kpeT[:, :]), banks)

                def uq(k, lo, n):
                    row = slot(ids["uq"][k // 2], 2 * 1536)[:, (k % 2) * 1536:(k % 2 + 1) * 1536]
                    if n:
                        return row[:, lo:lo + n]
                    return row.rearrange("p (h f) -> p h f", f=NOPE + ROPE)[:, :, NOPE:NOPE + ROPE]

                jobs = []
                for t in range(NT):
                    mms = [((P, 0, 512), cqT[:, k, t * P:(t + 1) * P], uq(k, 0, 0), k == 0, k == 3, False,
                            ids["uq"][k // 2]) for k in range(4)]
                    ev, on = turn(t, qpe[:, t, :], MLA_SCALE if s else None)
                    jobs.append(Job(mms, ev, on))
                for hh in range(MLA_HEADS):
                    mms = [((P, 0, S), uq(k, hh * (NOPE + ROPE), NOPE), cqT[:, k, :], k == 0, k == 3, False,
                            ids["uq"][k // 2]) for k in range(4)]
                    ev, on = turn(hh, qT[:, hh, :], MLA_SCALE, None, S)
                    jobs.append(Job(mms, ev, on, ids["uq"] if hh == MLA_HEADS - 1 else ()))
                self.run_uq = Run(jobs, banks)
                jobs = []
                for hh in range(MLA_HEADS):
                    mms = [((P, 0, S), slot(ids["ukv"][k], 2 * D)[:, 256 * hh:256 * hh + P], ckvT[:, k, :], k == 0, k == 1,
                            False, ids["ukv"][k]) for k in range(2)]
                    ev, on = turn(hh, kT[:, hh, :], None, None, S)
                    jobs.append(Job(mms, ev, on))
                for t in range(NT):
                    for half in range(2):
                        def wv(k, half=half):
                            return slot(ids["ukv"][k], 2 * D).rearrange("p (h f) -> p h f", f=256)[:, 4 * half:4 * half + 4, P:256]
                        mms = [((P, 0, 512), ckvT[:, k, t * P:(t + 1) * P], wv(k), k == 0, k == 1, False, ids["ukv"][k])
                               for k in range(2)]
                        ev, on = turn(half, va[:, t, 512 * half:512 * half + 512])
                        jobs.append(Job(mms, ev, on, ids["ukv"] if (t, half) == (1, 1) else ()))
                self.run_ukv = Run(jobs, banks)
                self.run_q = Run(transposes(4, lambda t, c: qpe[:, t, c * P:(c + 1) * P], lambda c: qpeT[:, c, :]), banks)
                self.a = Steps(sem(f"{name}_act"), rms_names(4))
                self.v = Steps(sem(f"{name}_dve"), ["var", "norms"] + ["rope_q"] * (s == 0))

                self.o = view(hT, NT, D)
                units = []
                nq = 1 if s == 0 else NT
                for hh in range(MLA_HEADS):
                    lo = HD * (hh % 2)
                    for t0 in range(0, NT, nq):
                        sc = []
                        for t in range(nq):
                            tt = t0 + t
                            sets = [(kT, kpeT)] if s else [(kTc, kpeTc), (kT, kpeT)]
                            for n, (keys, rot) in enumerate(sets):
                                at = (n + t) * S
                                sc.append((at, at + S, qT[:, hh, tt * P:(tt + 1) * P], keys[:, hh, :], True, False))
                                sc.append((at, at + S, qpeT[lo:lo + HD, hh // 2, tt * P:(tt + 1) * P],
                                           rot[lo:lo + HD, :], False, True))

                        def values(c, hh=hh):
                            tile = vac if s or c < NT else va
                            return tile[:, c % NT, P * hh:P * hh + P]
                        units.append({"nt": nq, "scores": sc, "v": values,
                                      "out": lambda t, hh=hh, t0=t0: self.o[:, t0 + t, P * hh:P * hh + P]})
                fill = None
                if s == 0:
                    base = ada_done.take(16)
                    fill = lambda pe, u: ada_piece(pe, 1, u, base)
                self.att = Attention(name, units, cq, view(cqT, 2, 512), fill=fill, bank=banks[0])

            def rope(self, dve, y, groups, table, t):
                v5 = y.rearrange("p (g a b f) -> p g a b f", g=groups, a=2, b=2)
                x1, x2 = (v5[:, :, :, b, :] for b in range(2))

                def tab(n):
                    z = cst[:, C_ROPE + 64 * (2 * table + n):][:, 32 * t:32 * t + 32]
                    return z.rearrange("p (o a f) -> p o a f", o=1, a=2).to_broadcast([P, groups, 2, 16])
                rot = view(self.buf["cqT"], 4, 256)

                def r(i):
                    return rot[:, i, 0:groups * 32].rearrange("p (g a f) -> p g a f", g=groups, a=2)
                for i, (z, n) in enumerate(((x1, 0), (x2, 1), (x1, 1), (x2, 0))):
                    last = nc.vector.tensor_tensor(r(i), z, tab(n), ALU.mult)
                link(dve, last)
                nc.vector.tensor_tensor(x1, r(0), r(1), ALU.subtract)
                return nc.vector.tensor_tensor(x2, r(2), r(3), ALU.add)

            def act_down(self, act):
                cq, ckv = self.buf["cq"], self.buf["ckv"]
                self.run_t.ev(act, "act")
                self.run_d.ev(act, "act")
                self.run_d.finished(act)
                rms_act(act, self.a, self.v, [cq[:, 0, :], cq[:, 1, :], ckv[:, 0, 0:KV_RANK], ckv[:, 1, 0:KV_RANK]],
                        view(self.buf["cqT"], 1, 1024)[:, 0, :], 0)
                self.run_c.ev(act, "act")

            def act_up(self, act):
                self.run_uq.ev(act, "act")
                self.run_ukv.ev(act, "act")
                self.run_q.ev(act, "act")

            def dve_down(self, dve):
                cq, ckv, kpe, v = self.buf["cq"], self.buf["ckv"], self.buf["kpe"], self.v
                self.run_t.ev(dve, "dve")
                self.run_d.ev(dve, "dve")
                self.run_d.finished(dve)
                rms_dve(dve, self.a, v, [(NT, Q_RANK, 1e-6), (NT, KV_RANK, 1e-6)], 0)
                for t in range(NT):
                    nc.vector.tensor_scalar(cq[:, t, :], cq[:, t, :], small[:, t:t + 1], None, ALU.mult)
                    nc.vector.tensor_scalar(ckv[:, t, 0:KV_RANK], ckv[:, t, 0:KV_RANK], small[:, 2 + t:3 + t],
                                            None, ALU.mult)
                    if self.s == 0:
                        link(dve, self.rope(dve, ckv[:, t, KV_RANK:], 1, 1, t))
                    src = ckv[:, t, KV_RANK:].rearrange("p (o f) -> p o f", o=1).to_broadcast([P, 2, ROPE])
                    last = nc.vector.tensor_copy(kpe[:, t, :].rearrange("p (o f) -> p o f", o=2), src)
                last.then_inc(v.sem, v("norms"))
                self.run_c.ev(dve, "dve")

            def dve_up(self, dve):
                self.run_uq.ev(dve, "dve")
                self.run_ukv.ev(dve, "dve")
                self.run_uq.finished(dve)
                if self.s == 0:
                    for t in range(NT):
                        last = self.rope(dve, self.buf["qpe"][:, t, :], MLA_HEADS, 0, t)
                        if t + 1 < NT:
                            link(dve, last)
                    last.then_inc(self.v.sem, self.v("rope_q"))
                self.run_q.ev(dve, "dve")

            def pe_down(self, pe):
                self.run_t.finished(pe)
                self.run_d.pe(pe)

            def pe_norm(self, pe):
                self.run_d.finished(pe)
                pe.wait_ge(self.v.sem, self.v.at("norms"))
                self.run_c.pe(pe)

            def pe_q(self, pe):
                self.run_c.finished(pe)
                self.run_uq.pe(pe)

            def pe_kv(self, pe):
                self.run_uq.finished(pe)
                self.run_ukv.pe(pe)

            def pe_turned(self, pe):
                self.run_ukv.finished(pe)
                if self.s == 0:
                    pe.wait_ge(self.v.sem, self.v.at("rope_q"))
                self.run_q.pe(pe)

        ex = ExitStack()
        xe = sb("xe", [KC, CAP], ex)
        gs = sb("gs", [S], ex)
        ye = sb("expert_work", [D], ex)
        eg = hg = hgT = ye
        stats = sb("stats_c", [NT, 14], ex)
        buf = {"hT": hT, "qT": view(h, KC, S), "qpe": sb("c_qpe", [NT, 512], ex), "qpeT": sb("c_qpeT", [4, S], ex)}
        early_qpe = view(buf["qpe"], 1, D)[:, 0, :]
        w = NT * (KV_RANK + ROPE)
        buf["ckv"] = early_qpe[:, 0:w].rearrange("p (t f) -> p t f", t=NT)
        buf["kpe"] = early_qpe[:, w:w + NT * 2 * ROPE].rearrange("p (t f) -> p t f", t=NT)
        buf["ckvT"] = buf["qpeT"][:, 0:2, :]
        pair_buf = sb("c_cq", [4, 512], ex)
        buf["cq"] = pair_buf[:, 0:2, :]
        buf["cqT"] = pair_buf[:, 2:4, :].rearrange("p a b -> p (a b)").rearrange("p (k s) -> p k s", k=4)
        lnb = view(pair_buf, 2, D)
        gB = view(buf["qpe"], 1, D)[:, 0, :]
        m_relu, m_h1 = view(buf["qT"], 4, 512)[:, 0:2, :], view(buf["qT"], 4, 512)[:, 2:4, :]
        CB = (4, 5, 6, 7)
        lat = LatentAttention(1, ids_c, buf, CB)
        run_g1 = Run(gate_jobs(0, 2, 1, gB), CB)
        run_oT = Run(transposes(KC, lambda t, c: lat.o[:, t, c * P:(c + 1) * P], lambda c: buf["qT"][:, c, :]), CB)
        run_wo = Run(square_jobs(buf["qT"], ids_c["o"], 1, gB), CB)
        run_g2 = Run(gate_jobs(0, 5, 1, gB), CB)
        run_mT = Run(modulated(0, 3, 1, buf["hT"]), CB)
        ca = Steps(sem("ctx_act"), ["ln_sd", "ln_sd2"])
        cv = Steps(sem("ctx_dve"), ["ln_var", "normed", "ln_var2"])
        moe_used = sem("moe_piece_used")
        xe_ready, gs_ready = sem("xe_ready"), sem("gs_ready")
        e_exp, e_h, e_tr, e_trA, e_trV = (sem(f"moe_{n}") for n in ("exp", "h", "tr", "trA", "trV"))
        e_yA, e_yV, e_sc, e_add = sem("moe_yA"), sem("moe_yV"), sem("moe_scattered"), sem("moe_added")
        c_used, c_relu, c_square = sem("ctx_mlp_used"), sem("ctx_relu"), sem("ctx_square")

        def expert_pe(pe, e, piece, used, between):
            pe.wait_ge(xe_ready, e + 1)
            pe.wait_ge(e_add, e + 1)
            for i in range(2 * KC):
                k, up = divmod(i, 2)
                w = piece(i)[:, 0:D_FF].rearrange("p (c f) -> p c f", f=P)
                for j in range(4):
                    nc.tensor.matmul(ps[32 * j:32 * j + 32, up, :], xe[:, k, :], w[:, j:j + 13:4, :],
                                     start=(k == 0), stop=(k == KC - 1))
                for j in range(4):
                    two = w[:, 16 + j:21 + j:4, :] if j < 2 else w[:, 16 + j:19 + j:2, :]
                    last = nc.tensor.matmul(ps[32 * j:32 * j + 32, 2, 256 * up:256 * up + 256], xe[:, k, :], two,
                                            start=(k == 0 and not up), stop=(k == KC - 1), skip_group_check=True)
                last.then_inc(moe_used, 1)
                used(i)
                between(i)
            pe.wait_ge(e_h, e + 1)
            for i in range(6):
                n = P if i < 5 else 64
                at = ps[:, 3, P * i:P * i + n] if i < 4 else ps[:, 0, P * (i - 4):P * (i - 4) + n]
                last = nc.tensor.transpose(at, hg[0:n, P * i:P * i + P], cst[0:n, C_ID:C_ID + n])
            last.then_inc(e_tr, 1)
            pe.wait_ge(e_trA, e + 1)
            pe.wait_ge(e_trV, e + 1)
            for i in range(2 * KC, PIECES):
                w = piece(i)
                c0 = 3 * (i - 2 * KC)
                for half in range(2):
                    for c in range(c0, min(c0 + 3, FCH)):
                        j = c % 4
                        last = nc.tensor.matmul(ps[32 * j:32 * j + 32, 1 + half, :],
                                                hgT[:, P * (c // 4) + 32 * j:P * (c // 4) + 32 * j + 32],
                                                w[:, (c - c0) * D + 512 * half:(c - c0) * D + 512 * half + 512],
                                                start=(c < 4), stop=(c >= FCH - 4))
                last.then_inc(moe_used, 1)
                used(i)
            pe.wait_ge(gs_ready, e + 1)
            pe.wait_ge(e_yA, e + 1)
            pe.wait_ge(e_yV, e + 1)
            for t in range(NT):
                for half in range(2):
                    last = nc.tensor.matmul(ps[:, 2 * t + half, :], gs[:, t * P:(t + 1) * P],
                                            ye[:, 512 * half:512 * half + 512], start=True, stop=True)
            last.then_inc(e_sc, 1)

        def expert_act(act, e):
            act.wait_ge(moe_used, e * PIECES + 2 * KC)
            nc.scalar.activation(eg[:, 0:512], ps[:, 0, :], ACT.Exp, scale=-1.0)
            nc.scalar.activation(eg[:, 512:768], ps[:, 2, 0:256], ACT.Exp, scale=-1.0).then_inc(e_exp, 1)
            act.wait_ge(e_tr, e + 1)
            nc.scalar.activation(hgT[:, 0:512], ps[:, 3, :], ACT.Identity).then_inc(e_trA, 1)
            act.wait_ge(moe_used, e * PIECES + PIECES)
            nc.scalar.activation(ye[:, 0:512], ps[:, 1, :], ACT.Identity).then_inc(e_yA, 1)

        def expert_dve(dve, e):
            dve.wait_ge(e_exp, e + 1)
            nc.vector.tensor_scalar(eg[:, 0:768], eg[:, 0:768], 1.0, None, ALU.add).then_inc(e_own, 1)
            dve.wait_ge(e_own, e * 4 + 1)
            nc.vector.reciprocal(eg[:, 0:768], eg[:, 0:768]).then_inc(e_own, 1)
            dve.wait_ge(e_own, e * 4 + 2)
            nc.vector.tensor_tensor(eg[:, 0:512], ps[:, 0, :], eg[:, 0:512], ALU.mult).then_inc(e_own, 1)
            nc.vector.tensor_tensor(eg[:, 512:768], ps[:, 2, 0:256], eg[:, 512:768], ALU.mult).then_inc(e_own, 1)
            dve.wait_ge(e_own, e * 4 + 4)
            nc.vector.tensor_tensor(hg[:, 0:512], ps[:, 1, :], eg[:, 0:512], ALU.mult)
            nc.vector.tensor_tensor(hg[:, 512:768], ps[:, 2, 256:512], eg[:, 512:768], ALU.mult).then_inc(e_h, 1)
            dve.wait_ge(e_tr, e + 1)
            nc.vector.tensor_copy(hgT[:, 512:704], ps[:, 0, 0:192]).then_inc(e_trV, 1)
            dve.wait_ge(moe_used, e * PIECES + PIECES)
            nc.vector.tensor_copy(ye[:, 512:1024], ps[:, 2, :]).then_inc(e_yV, 1)
            dve.wait_ge(e_sc, e + 2)
            for t in range(NT):
                last = nc.vector.tensor_tensor(x[:, t, :], ps[:, 2 * t:2 * t + 2, :].rearrange("p b f -> p (b f)"),
                                               x[:, t, :], ALU.add)
            last.then_inc(e_add, 1)

        with nc.Block(no_gpsimd_drain=True) as block:
            @block.tensor
            def _(pe):
                def attention_front(pe):
                    lat.run_q.finished(pe)
                    yield from lat.att.pe_units(pe)

                units = attention_front(pe)

                def context(e, i):
                    at = (e, i)
                    if at == (0, 1):
                        pe.wait_ge(cx_loaded, 16)
                        lat.run_t.pe(pe)
                    elif at == (0, 4):
                        lat.pe_down(pe)
                    elif at == (0, 11):
                        lat.pe_norm(pe)
                    elif at == (1, 2):
                        lat.pe_q(pe)
                    elif at == (1, 8):
                        lat.pe_kv(pe)
                    elif at == (1, 13):
                        lat.pe_turned(pe)
                    elif e == 2 and i % 2 == 1:
                        next(units)
                        if i == 15:
                            next(units, None)
                    elif at == (3, 2):
                        lat.att.finished(pe)
                        run_g1.pe(pe)
                        run_g1.finished(pe)
                        run_oT.pe(pe)
                    elif at == (3, 6):
                        run_oT.finished(pe)
                        run_wo.pe(pe)
                    elif at == (4, 8):
                        run_wo.finished(pe)
                        pe.wait_ge(cv.sem, cv.at("normed"))
                        run_g2.pe(pe)
                        run_g2.finished(pe)
                        run_mT.pe(pe)
                    elif at == (4, 12):
                        run_mT.finished(pe)
                        for b in CB:
                            nc.tensor.matmul(ps[:, b, :], zeros[:, :], cst[:, 0:512], start=True, stop=True)

                def straight(e):
                    def piece(i):
                        arrived(pe, moe_ids[e, i])
                        return slot(moe_ids[e, i], SLOT)

                    def used(i):
                        released[moe_ids[e, i]] = (moe_used, e * PIECES + i + 1)
                    expert_pe(pe, e, piece, used, lambda i: context(e, i))

                for e in range(LEAD):
                    straight(e)
                with pe.Fori(0, PAIRS) as m:
                    for d in range(2):
                        def piece(i):
                            return slot(pairs.arrived(pe, m, pair_at[d, i]), SLOT)

                        def used(i):
                            pairs.uses(pair_at[d, i], moe_used, (LEAD + d) * PIECES + i + 1, 2 * PIECES)

                        def mlp_part(i):
                            if i not in MLP_AFTER:
                                return
                            w, g = MLP_AFTER[i]
                            n = pairs.arrived(pe, m, pair_at[d, "mlp", i])
                            if w == 1:
                                w1 = slot(n, KC * 2 * P).rearrange("p (k f) -> p k f", k=KC)
                                if g:
                                    pe.wait_ge(c_relu, m * 4 + (2 * d + 1))
                                for fc in range(2):
                                    for k in range(KC):
                                        last = nc.tensor.matmul(ps[:, 3, S * fc:S * fc + S], w1[:, k, fc * P:(fc + 1) * P],
                                                                buf["hT"][:, k, :], start=(k == 0), stop=(k == KC - 1))
                            else:
                                pe.wait_ge(c_square, m * 4 + (2 * d + g + 1))
                                w2 = slot(n, 2 * D).rearrange("p (k f) -> p k f", k=2)
                                for t in range(NT):
                                    for half in range(2):
                                        for fc in range(2):
                                            last = nc.tensor.matmul(ps[:, CB[2 * t + half], :],
                                                                    m_h1[:, g, S * fc + t * P:S * fc + (t + 1) * P],
                                                                    w2[:, fc, 512 * half:512 * half + 512],
                                                                    start=False, stop=True, skip_group_check=True)
                            last.then_inc(c_used, 1)
                            pairs.uses(pair_at[d, "mlp", i], c_used, 4 * d + 2 * g + w, 8)
                        expert_pe(pe, m * 2 + (LEAD + d), piece, used, mlp_part)
                pairs.end()
                straight(AFTER_PAIRS)
                with pe.Fori(0, N_EXPERTS - FINAL) as m:
                    def piece(i):
                        return slot(finals.arrived(pe, m, i), SLOT)

                    def used(i):
                        finals.uses(i, moe_used, FINAL * PIECES + i + 1, PIECES)
                    expert_pe(pe, m + FINAL, piece, used, lambda i: None)
                finals.end()

            @block.sync
            def _(sp):
                feed(sp)
                pairs.feed(sp)
                feed(sp)
                finals.feed(sp)
                feed(sp)

            @block.gpsimd
            def _(pool):
                with pool.Fori(0, N_EXPERTS) as e:
                    pool.wait_ge(e_sc, e + 1)
                    nc.gpsimd.tensor_copy(xe[:, :, :], xeT[:, :, bass.ds(e * CAP, CAP)]).then_inc(xe_ready, 1)
                    nc.gpsimd.tensor_copy(gs[:, :], gT[:, bass.ds(e, 1), :].rearrange("p o s -> p (o s)")).then_inc(gs_ready, 1)

            @block.scalar
            def _(act):
                nc.scalar.activation(small[:, 63:64], zeros[:, 0:1], ACT.Identity).then_inc(e_sc, 1)
                lat.act_down(act)
                expert_act(act, 0)
                lat.act_up(act)
                expert_act(act, 1)
                lat.att.act(act)
                expert_act(act, 2)
                lat.att.finished(act)
                load_ln(act, 1, 0, lnb)
                run_g1.ev(act, "act")
                run_oT.ev(act, "act")
                ln_act(act, ca, cv)
                expert_act(act, 3)
                act.wait_ge(cv.sem, cv.at("normed"))
                load_ln(act, 2, 0, lnb)
                run_g2.ev(act, "act")
                run_mT.ev(act, "act")
                expert_act(act, 4)
                with act.Fori(0, PAIRS) as m:
                    for d in range(2):
                        for g in range(2):
                            act.wait_ge(c_used, m * 8 + (4 * d + 2 * g + 1))
                            nc.scalar.activation(m_relu[:, g, :], ps[:, 3, :], ACT.Relu).then_inc(c_relu, 1)
                        expert_act(act, m * 2 + (LEAD + d))
                ln_act(act, ca, cv, "2")
                expert_act(act, AFTER_PAIRS)
                with act.Fori(0, N_EXPERTS - FINAL) as m:
                    expert_act(act, m + FINAL)

            @block.vector
            def _(dve):
                nc.vector.memset(small[:, 61:62], 0.0).then_inc(e_add, 1)
                lat.dve_down(dve)
                expert_dve(dve, 0)
                lat.dve_up(dve)
                expert_dve(dve, 1)
                lat.att.dve(dve, dve_own, dve_count)
                expert_dve(dve, 2)
                run_g1.ev(dve, "dve")
                run_g1.finished(dve)
                run_oT.ev(dve, "dve")
                run_wo.ev(dve, "dve")
                run_wo.finished(dve)
                dve.wait_ge(ln_loaded.sem, 32)
                ln_dve(dve, ca, cv, cx, lnb[:, 0, :], lnb[:, 1, :], stats)
                nc.vector.memset(small[:, 62:63], 0.0).then_inc(cv.sem, cv("normed"))
                expert_dve(dve, 3)
                run_g2.ev(dve, "dve")
                run_mT.ev(dve, "dve")
                expert_dve(dve, 4)
                with dve.Fori(0, PAIRS) as m:
                    for d in range(2):
                        for g in range(2):
                            dve.wait_ge(c_relu, m * 4 + (2 * d + g + 1))
                            nc.vector.tensor_tensor(m_h1[:, g, :], m_relu[:, g, :], m_relu[:, g, :], ALU.mult)\
                              .then_inc(c_square, 1)
                        expert_dve(dve, m * 2 + (LEAD + d))
                dve.wait_ge(c_used, 8 * PAIRS)
                run_g2.finished(dve)
                for t in range(NT):
                    for half in range(2):
                        last = gated(ps[:, CB[2 * t + half], :], cx[:, t, 512 * half:512 * half + 512],
                                     gB[:, 512 * half:512 * half + 512])
                link(dve, last)
                dve.wait_ge(ln_loaded.sem, 64)
                ln_dve(dve, ca, cv, cx, lnb[:, 0, :], lnb[:, 1, :], stats, "2")
                expert_dve(dve, AFTER_PAIRS)
                with dve.Fori(0, N_EXPERTS - FINAL) as m:
                    expert_dve(dve, m + FINAL)
        ex.close()
        keep.close()
        first.close()

        second = ExitStack()
        gB = sb("gB", [D], second)
        lnb = sb("lnb", [2, D], second)
        stats = sb("stats", [NT, 14], second)
        af, vf = Steps(sem("pf_act"), rms_names(NT)), Steps(sem("pf_dve"), ["var"])
        with nc.Block(no_gpsimd_drain=True) as block:
            @block.scalar
            def _(act):
                act.dma_start(lnb[:, 0, :], A["norm_f_g"].partition_broadcast(P)).then_inc(ln_loaded.sem, 16)
                ln_loaded.take(16)
                rms_act(act, af, vf, [x[:, t, :] for t in range(NT)], gB, 0)

            @block.sync
            def _(sp):
                feed(sp)

            @block.vector
            def _(dve):
                rms_dve(dve, af, vf, [(NT, D, 1e-6)], 0)
                dve.wait_ge(ln_loaded.sem, ln_loaded.n)
                for t in range(NT):
                    nc.vector.scalar_tensor_tensor(x[:, t, :], x[:, t, :], small[:, t:t + 1], lnb[:, 0, :], ALU.mult, ALU.mult)

        def mixer_end(name, layer, s, o, oT, where, before=None):
            pre, act_pre, dve_pre, dve_post = before or ([], None, None, None)
            run_pre = Run(pre)
            run_gate = Run(gate_jobs(layer, 2, s, gB), (4, 5))
            run_t = Run(transposes(KC, lambda t, c: o[:, t, c * P:(c + 1) * P], lambda c: oT[:, c, :]))
            run_w = Run(square_jobs(oT, where, s, gB), (4, 5, 6, 7))
            a, v = Steps(sem(f"{name}_act"), ["pre", "ln_sd"]), Steps(sem(f"{name}_dve"), ["pre", "ln_var"])
            with nc.Block(no_gpsimd_drain=True) as block:
                @block.tensor
                def _(pe):
                    pe.wait_ge(a.sem, a.at("pre"))
                    pe.wait_ge(v.sem, v.at("pre"))
                    run_pre.pe(pe)
                    run_pre.finished(pe)
                    run_gate.pe(pe)
                    run_gate.finished(pe)
                    run_t.pe(pe)
                    run_t.finished(pe)
                    run_w.pe(pe)

                @block.sync
                def _(sp):
                    feed(sp)

                @block.scalar
                def _(act):
                    load_ln(act, 1, layer, lnb)
                    last = act_pre() if act_pre else nc.scalar.activation(small[:, 60:61], zeros[:, 0:1], ACT.Identity)
                    last.then_inc(a.sem, a("pre"))
                    run_gate.ev(act, "act")
                    run_t.ev(act, "act")
                    ln_act(act, a, v)

                @block.vector
                def _(dve):
                    last = dve_pre() if dve_pre else nc.vector.memset(small[:, 61:62], 0.0)
                    last.then_inc(v.sem, v("pre"))
                    run_pre.ev(dve, "dve")
                    run_pre.finished(dve)
                    if dve_post:
                        dve_post(dve)
                    run_gate.ev(dve, "dve")
                    run_t.ev(dve, "dve")
                    run_gate.finished(dve)
                    run_w.ev(dve, "dve")
                    run_w.finished(dve)
                    dve.wait_ge(ln_loaded.sem, ln_loaded.n)
                    ln_dve(dve, a, v, streams[s], lnb[:, 0, :], lnb[:, 1, :], stats)

        def mlp(name, layer, s, loop):
            st = ExitStack()
            hT = sb(f"{name}_hT", [KC, S], st)
            relu = sb(f"{name}_relu", [2, 2 * S], st)
            h1 = sb(f"{name}_h1", [2, 2, S], st)
            run_gate = Run(gate_jobs(layer, 5, s, gB), (4, 5))
            run_t = Run(modulated(layer, 3, s, hT))
            a, v = Steps(sem(f"{name}_act"), ["ln_sd"]), Steps(sem(f"{name}_dve"), ["ln_var"])
            used = mlp_used.take(8 * GROUPS // TURN)
            rb, qb = relu_done.take(GROUPS), square_done.take(GROUPS)
            turns = GROUPS // TURN
            pos = {wg: i + 1 for i, wg in enumerate(ORDER)}
            with nc.Block(no_gpsimd_drain=True) as block:
                @block.tensor
                def _(pe):
                    run_gate.pe(pe)
                    run_t.pe(pe)
                    run_gate.finished(pe)
                    run_t.finished(pe)
                    for b in range(4):
                        nc.tensor.matmul(ps[:, 4 + b, :], zeros[:, :], cst[:, 0:512], start=True, stop=True)
                    with pe.Fori(0, turns) as m:
                        for i, (w, g) in enumerate(ORDER):
                            n = loop.arrived(pe, m, i)
                            if w == 1:
                                w1 = slot(n, KC * 2 * P).rearrange("p (k f) -> p k f", k=KC)
                                for fc in range(2):
                                    for k in range(KC):
                                        last = nc.tensor.matmul(ps[:, g % 2, S * fc:S * fc + S],
                                                                w1[:, k, fc * P:(fc + 1) * P], hT[:, k, :],
                                                                start=(k == 0), stop=(k == KC - 1))
                            else:
                                pe.wait_ge(square_done.sem, m * TURN + (qb + g + 1))
                                w2 = slot(n, 2 * D).rearrange("p (k f) -> p k f", k=2)
                                for t in range(NT):
                                    for half in range(2):
                                        for fc in range(2):
                                            last = nc.tensor.matmul(ps[:, 4 + 2 * t + half, :],
                                                                    h1[:, g % 2, fc, t * P:(t + 1) * P],
                                                                    w2[:, fc, 512 * half:512 * half + 512],
                                                                    start=False, stop=True, skip_group_check=True)
                            last.then_inc(mlp_used.sem, 1)
                            loop.uses(i, mlp_used.sem, used + i + 1, 8)
                    loop.end()

                @block.sync
                def _(sp):
                    feed(sp)
                    loop.feed(sp)
                    feed(sp)

                @block.scalar
                def _(act):
                    load_ln(act, 2, layer, lnb)
                    run_gate.ev(act, "act")
                    run_t.ev(act, "act")
                    with act.Fori(0, turns) as m:
                        for g in range(TURN):
                            act.wait_ge(mlp_used.sem, m * 8 + (used + pos[1, g]))
                            nc.scalar.activation(relu[:, g % 2, :], ps[:, g % 2, :], ACT.Relu).then_inc(relu_done.sem, 1)
                    ln_act(act, a, v)

                @block.vector
                def _(dve):
                    run_gate.ev(dve, "dve")
                    run_t.ev(dve, "dve")
                    run_gate.finished(dve)
                    with dve.Fori(0, turns) as m:
                        for g in range(TURN):
                            dve.wait_ge(relu_done.sem, m * TURN + (rb + g + 1))
                            nc.vector.tensor_tensor(h1[:, g % 2, :, :].rearrange("p a b -> p (a b)"), relu[:, g % 2, :],
                                                    relu[:, g % 2, :], ALU.mult).then_inc(square_done.sem, 1)
                    dve.wait_ge(mlp_used.sem, used + 8 * turns)
                    for t in range(NT):
                        for half in range(2):
                            last = gated(ps[:, 4 + 2 * t + half, :], streams[s][:, t, 512 * half:512 * half + 512],
                                         gB[:, 512 * half:512 * half + 512])
                    link(dve, last)
                    dve.wait_ge(ln_loaded.sem, ln_loaded.n)
                    ln_dve(dve, a, v, streams[s], lnb[:, 0, :], lnb[:, 1, :], stats)
            st.close()

        st = ExitStack()
        buf = {k: sb(f"x_{k}", shape, st) for k, shape in
               {"hT": [KC, S], "qT": [MLA_HEADS, S], "cq": [NT, Q_RANK], "ckv": [NT, KV_RANK + ROPE], "kpe": [NT, 2 * ROPE],
                "cqT": [4, S], "ckvT": [2, S], "qpe": [NT, 512], "qpeT": [4, S], "kT": [KC, S], "kpeT": [S],
                "va": [NT, D]}.items()}
        lat = LatentAttention(0, ids_x, buf, (0, 1, 2, 3))
        with nc.Block(no_gpsimd_drain=True) as block:
            @block.tensor
            def _(pe):
                lat.run_t.pe(pe)
                lat.pe_down(pe)
                lat.pe_norm(pe)
                lat.pe_q(pe)
                lat.pe_kv(pe)
                lat.pe_turned(pe)
                lat.run_q.finished(pe)
                lat.att.pe(pe)

            @block.sync
            def _(sp):
                feed(sp)

            @block.scalar
            def _(act):
                lat.act_down(act)
                lat.act_up(act)
                lat.att.act(act)

            @block.vector
            def _(dve):
                lat.dve_down(dve)
                lat.dve_up(dve)
                lat.att.dve(dve, dve_own, dve_count)

        rows1 = view(buf["qT"], 4, 512)

        def act_pre():
            row_out(0, rows1, 128, "act")
            return row_out(2, rows1, 128, "act")

        def dve_pre():
            row_out(1, rows1, 64, "dve")
            return row_out(3, rows1, 64, "dve")

        def dve_post(dve):
            for i in (1, 4):
                part = modc[:, 1, 8 * i:8 * i + 8, :]
                link(dve, nc.vector.tensor_scalar(part, part, 1.0, None, ALU.add))
        mixer_end("mla0_end", 0, 0, lat.o, buf["qT"], ids_x["o"], (ada_jobs(1, rows1), act_pre, dve_pre, dve_post))
        st.close()
        mlp("mlp_x", 0, 0, mlp_x)

        st = ExitStack()
        kT = sb("na_kT", [KC, 2 * S], st)
        va_x = sb("na_v", [NT, D], st)
        va = lambda t: (vac if t < NT else va_x)[:, t % NT, :]
        hT2 = sb("na_hT", [KC, 2 * S], st)
        qT = kTc
        vb = gB
        naw = sb("na_window", [NA_HEADS, NA_WIN], st)
        na_loaded = sem("na_loaded")
        run_tc = Run(modulated(1, 0, 1, hT2, 0) + modulated(1, 0, 0, hT2, S))
        jobs = []
        for n in range(KC):
            mms = [((P, 0, S), slot(id_na[k], N_IN)[:, n * P:(n + 1) * P], hT2[:, k, S:2 * S], k == 0, k == KC - 1, False,
                    id_na[k]) for k in range(KC)]

            def ev(bank, n=n):
                return nc.vector.tensor_scalar(qT[:, n, :], bank[:, 0:S], vc(V_BQKV + n), HD ** -0.5, ALU.add, ALU.mult)
            jobs.append(Job(mms, ev, "dve"))
        for n in range(KC):
            mms = [((P, 0, 2 * S), slot(id_na[k], N_IN)[:, D + n * P:D + (n + 1) * P], hT2[:, k, :], k == 0, k == KC - 1,
                    False, id_na[k]) for k in range(KC)]
            ev, on = turn(n, kT[:, n, :], None, vc(V_BQKV + KC + n))
            jobs.append(Job(mms, ev, on))
        for t in range(2 * NT):
            for half in range(2):
                mms = [((P, 0, 512), hT2[:, k, t * P:(t + 1) * P],
                        slot(id_na[k], N_IN)[:, 2 * D + 512 * half:2 * D + 512 * half + 512], k == 0, k == KC - 1, False,
                        id_na[k]) for k in range(KC)]

                def ev(bank, t=t, half=half):
                    return nc.vector.tensor_tensor(va(t)[:, 512 * half:512 * half + 512], bank,
                                                   vb[:, 512 * half:512 * half + 512], ALU.add)
                jobs.append(Job(mms, ev, "dve", id_na if (t, half) == (3, 1) else ()))
        run_n = Run(jobs, (4, 5, 6, 7, 0, 1, 2, 3))
        with nc.Block(no_gpsimd_drain=True) as block:
            @block.tensor
            def _(pe):
                run_tc.pe(pe)
                run_tc.finished(pe)
                run_n.pe(pe)

            @block.sync
            def _(sp):
                feed(sp)

            @block.scalar
            def _(act):
                act.dma_start(vb[:, :], A["na_b_qkv_2"][0:1, 2 * D:3 * D].partition_broadcast(P)
                              .rearrange("q o d -> q (o d)")).then_inc(na_loaded, 16)
                rpb = A["na_rpb_2"]
                for par in range(2):
                    src = bass.AP(tensor=rpb.tensor, offset=rpb.offset + 4 * RPB_W + 15 + 31 * par - 63,
                                  ap=[[1, 64], [RPB_N, NA_HEADS], [1, NA_WIN]])
                    act.dma_start(naw[64 * par:64 * par + 64, :, :], src).then_inc(na_loaded, 16)
                run_tc.ev(act, "act")
                run_n.ev(act, "act")

            @block.vector
            def _(dve):
                run_tc.ev(dve, "dve")
                dve.wait_ge(na_loaded, 48)
                run_n.ev(dve, "dve")

        o = view(hT2, 4, D)[:, 0:NT, :]
        oT = view(hT2, 2 * KC, S)[:, KC:2 * KC, :]
        probs, probsT = (oT[:, 4 * i:4 * i + 4, :].rearrange("p k s -> p (k s)").rearrange("p (a b) -> p a b", a=2)
                         for i in range(2))
        units = []
        for hh in range(NA_HEADS):
            for t in range(NT):
                lo = HD * (hh % 2)
                win = naw[:, hh, RPB_W * (2 - 2 * t):RPB_W * (2 - 2 * t) + GRID_W]
                win = bass.AP(tensor=win.tensor, offset=win.offset, ap=[list(win.ap[0]), [RPB_W, 4], [1, GRID_W]])
                sc = [(0, 512, qT[lo:lo + HD, hh // 2, t * P:(t + 1) * P], kT[lo:lo + HD, hh // 2, :], True, False),
                      (S, 2 * S, flip, win, False, False),
                      (S, 2 * S, ident, cst[:, C_MASK:C_MASK + S], False, True)]
                units.append({"nt": 1, "scores": sc, "v": lambda c, hh=hh: va(c)[:, HD * hh:HD * hh + HD],
                              "out": lambda q, hh=hh, t=t: o[:, t, HD * hh:HD * hh + HD]})
        att = Attention("na", units, probs, probsT)
        with nc.Block(no_gpsimd_drain=True) as block:
            @block.tensor
            def _(pe):
                att.pe(pe)

            @block.sync
            def _(sp):
                feed(sp)

            @block.scalar
            def _(act):
                att.act(act)

            @block.vector
            def _(dve):
                att.dve(dve, dve_own, dve_count)
        mixer_end("na_end", 1, 0, o, oT, id_nao)
        st.close()
        stored = sem("stored")
        mlp("mlp_n", 1, 0, mlp_n)
        with nc.Block(no_gpsimd_drain=True) as block:
            @block.sync
            def _(sp):
                sp.dma_start(A["out"].rearrange("b (t p) d -> p (b t) d", p=P), x[:, :, :]).then_inc(stored, 16)
                sp.wait_ge(stored, 16)
        second.close()


_INS = ["x", "norm1_g", "w_in", "lam_q1", "lam_k1", "lam_q2", "lam_k2", "subln_g", "w_out", "rel_bias", "norm2_g",
        "w_router", "w_gate", "w_up", "w_down", "norm_f_g", "c_2", "ctx_2", "c_ctx_2", "ada_w_2", "ada_b_2",
        "ln1_g_2", "ln1_b_2", "ln2_g_2", "ln2_b_2", "mlp_w1_2", "mlp_w2_2", "mla_w_dq_2", "mla_q_norm_2",
        "mla_w_uq_2", "mla_w_dkv_2", "mla_kv_norm_2", "mla_w_ukv_2", "mla_w_o_2", "na_w_qkv_2", "na_b_qkv_2",
        "na_rpb_2", "na_w_o_2"]


def kernel(**inputs):
    import concourse.bacc as bacc
    from concourse.bass_utils import run_bass_kernel_spmd

    nc = bacc.Bacc("TRN2", target_bir_lowering=False, num_devices=1)
    arrays, aps = {}, {}
    for name in _INS:
        arrays[f"in_{name}"] = np.ascontiguousarray(inputs[name])
    for name, table in shape_constants().items():
        arrays[f"in_{name}"] = table
    for name, a in arrays.items():
        aps[name[3:]] = nc.dram_tensor(name, a.shape, mybir.dt.from_np(a.dtype), kind="ExternalInput").ap()
    aps["out"] = nc.dram_tensor("out", (1, S, D), F32, kind="ExternalOutput").ap()
    build(nc, aps)
    r = run_bass_kernel_spmd(nc, [arrays], core_ids=[0])
    return r.results[0]["out"]
```
